# Optimizing a Trainium2 kernel written in Bass

```python
import jax, jax.numpy as jnp
from jax import lax
import numpy as np

D_MODEL = 1024
BATCH = 1
SEQ = 512
DEPTH = 4
DEC_BATCH = 1
DEC_SEQ = 32
PAST_LEN = 256

CHUNK = 64
EPS = 1e-6
NEG_INF = -1e30
MIXER_PATTERN = ('gla', 'band_attn', 'rglru')

GLA_HEADS = 4
GLA_DK = D_MODEL // 2 // GLA_HEADS
GLA_DV = D_MODEL // GLA_HEADS
GLA_GATE_RANK = 16
GLA_GATE_TAU = 16.0
GLA_IN = 2 * GLA_HEADS * GLA_DK + 2 * GLA_HEADS * GLA_DV

ATT_HEADS = 16
ATT_DH = D_MODEL // ATT_HEADS
ATT_PREV_CHUNKS = 8
ATT_BAND = ATT_PREV_CHUNKS * CHUNK
ATT_MAX_REL = 128

LRU_WIDTH = ((4 * D_MODEL // 3 + 255) // 256) * 256
LRU_BLOCKS = 16
LRU_BLOCK = LRU_WIDTH // LRU_BLOCKS
CONV_WIDTH = 4
LRU_C = 8.0

D_FF = ((8 * D_MODEL // 3 + 255) // 256) * 256

kernel_name = 'hybrid_streaming_encoder_step'

def rmsnorm(x, g):
    xf = x.astype(jnp.float32)
    y = xf * lax.rsqrt(jnp.mean(xf * xf, axis=-1, keepdims=True) + EPS)
    return (y * g.astype(jnp.float32)).astype(x.dtype)

def swiglu_ffn(x, w_in, w_out):
    g, u = jnp.split(x @ w_in, 2, axis=-1)
    return (jax.nn.silu(g) * u) @ w_out

def gla_chunk(S, xs):
    qc, kc, vc, gc = xs
    C = qc.shape[2]
    b = jnp.cumsum(gc, axis=2)
    q_e = qc * jnp.exp(b)
    k_e = kc * jnp.exp(-b)
    causal = jnp.tril(jnp.ones((C, C), dtype=bool))
    a = jnp.where(causal, jnp.einsum('bhtd,bhsd->bhts', q_e, k_e), 0.0)
    o = jnp.einsum('bhts,bhsv->bhtv', a, vc) + jnp.einsum('bhtd,bhdv->bhtv', q_e, S)
    b_last = b[:, :, -1:, :]
    S_new = jnp.exp(b_last[:, :, 0, :])[..., None] * S + jnp.einsum(
        'bhsd,bhsv->bhdv', kc * jnp.exp(b_last - b), vc)
    return S_new, o

def gla_mixer(h, S0, w_in, w_gate_a, w_gate_b, b_gate, head_norm, w_out):
    B, T, _ = h.shape
    hk, hv = GLA_HEADS * GLA_DK, GLA_HEADS * GLA_DV
    q, k, v, r = jnp.split(h @ w_in, [hk, 2 * hk, 2 * hk + hv], axis=-1)
    g = jax.nn.log_sigmoid(((h @ w_gate_a) @ w_gate_b + b_gate).astype(jnp.float32)) / GLA_GATE_TAU

    def heads(t, d):
        return t.reshape(B, T, GLA_HEADS, d).transpose(0, 2, 1, 3).astype(jnp.float32)

    q = heads(q, GLA_DK) * GLA_DK ** -0.5
    k = heads(k, GLA_DK)
    v = heads(v, GLA_DV)
    g = heads(g, GLA_DK)
    C = min(T, CHUNK)
    nc = T // C

    def to_chunks(t):
        return jnp.moveaxis(t.reshape(B, GLA_HEADS, nc, C, t.shape[-1]), 2, 0)

    S, o = lax.scan(gla_chunk, S0.astype(jnp.float32),
                    (to_chunks(q), to_chunks(k), to_chunks(v), to_chunks(g)))
    o = jnp.moveaxis(o, 0, 2).reshape(B, GLA_HEADS, T, GLA_DV)
    o = o * lax.rsqrt(jnp.mean(o * o, axis=-1, keepdims=True) + EPS) * head_norm.astype(jnp.float32)
    o = o.transpose(0, 2, 1, 3).reshape(B, T, hv).astype(h.dtype)
    y = (o * jax.nn.silu(r)) @ w_out
    return y, S.astype(h.dtype)

def rel_bias(table, dist):
    idx = jnp.clip(dist, -ATT_MAX_REL, ATT_MAX_REL) + ATT_MAX_REL
    return table[:, idx].astype(jnp.float32)

def attend(q, k, v, bias, valid):
    s = jnp.einsum('bqhd,bkhd->bhqk', q, k).astype(jnp.float32) * ATT_DH ** -0.5 + bias
    s = jnp.where(valid, s, NEG_INF)
    p = jax.nn.softmax(s, axis=-1).astype(v.dtype)
    return jnp.einsum('bhqk,bkhd->bqhd', p, v)

def qkv_heads(h, w_qkv):
    B, T, _ = h.shape
    q, k, v = jnp.split(h @ w_qkv, 3, axis=-1)
    return (q.reshape(B, T, ATT_HEADS, ATT_DH), k.reshape(B, T, ATT_HEADS, ATT_DH),
            v.reshape(B, T, ATT_HEADS, ATT_DH))

def band_attn_prompt(h, w_qkv, rel_table, w_out):
    B, T, _ = h.shape
    q, k, v = qkv_heads(h, w_qkv)
    nc = T // CHUNK
    band = ATT_BAND + CHUNK
    pad = ((0, 0), (ATT_BAND, 0), (0, 0), (0, 0))
    kp = jnp.pad(k, pad)
    vp = jnp.pad(v, pad)
    t_idx = jnp.arange(CHUNK)[:, None]
    r_idx = jnp.arange(band)[None, :]
    bias = rel_bias(rel_table, ATT_BAND + t_idx - r_idx)
    q_chunks = jnp.moveaxis(q.reshape(B, nc, CHUNK, ATT_HEADS, ATT_DH), 1, 0)

    def one_chunk(args):
        c, qc = args
        kb = lax.dynamic_slice_in_dim(kp, c * CHUNK, band, axis=1)
        vb = lax.dynamic_slice_in_dim(vp, c * CHUNK, band, axis=1)
        valid = r_idx[0] >= ATT_BAND - c * CHUNK
        return attend(qc, kb, vb, bias, valid)

    o = lax.map(one_chunk, (jnp.arange(nc), q_chunks))
    o = jnp.moveaxis(o, 0, 1).reshape(B, T, D_MODEL)
    keep = min(ATT_BAND, T)
    return o @ w_out, k[:, T - keep:], v[:, T - keep:]

def band_attn_sample(h, cache_k, cache_v, w_qkv, rel_table, w_out):
    B, T, _ = h.shape
    q, k, v = qkv_heads(h, w_qkv)
    P = cache_k.shape[1]
    kk = jnp.concatenate([cache_k.astype(k.dtype), k], axis=1)
    vv = jnp.concatenate([cache_v.astype(v.dtype), v], axis=1)
    bias = rel_bias(rel_table, P + jnp.arange(T)[:, None] - jnp.arange(P + T)[None, :])
    o = attend(q, kk, vv, bias, True)
    return o.reshape(B, T, D_MODEL) @ w_out, k, v

def linear_recurrence(a, u, h0):
    u = u.at[:, 0].add(a[:, 0] * h0)

    def combine(left, right):
        al, ul = left
        ar, ur = right
        return al * ar, ar * ul + ur

    _, hs = lax.associative_scan(combine, (a, u), axis=1)
    return hs

def rglru_mixer(h, h0, conv_buf, w_in, conv_w, conv_b, w_rgate, b_rgate, w_igate, b_igate, lam, w_out):
    B, T, _ = h.shape
    gate, xr = jnp.split(h @ w_in, 2, axis=-1)
    xpad = jnp.concatenate([conv_buf.astype(xr.dtype), xr], axis=1)
    xc = lax.conv_general_dilated(xpad, conv_w[:, None, :], window_strides=(1,), padding='VALID',
                                  dimension_numbers=('NWC', 'WIO', 'NWC'),
                                  feature_group_count=LRU_WIDTH) + conv_b
    new_buf = xpad[:, T:]
    xb = xc.reshape(B, T, LRU_BLOCKS, LRU_BLOCK)
    r = jax.nn.sigmoid((jnp.einsum('btni,nij->btnj', xb, w_rgate).reshape(B, T, LRU_WIDTH)
                        + b_rgate).astype(jnp.float32))
    i = jax.nn.sigmoid((jnp.einsum('btni,nij->btnj', xb, w_igate).reshape(B, T, LRU_WIDTH)
                        + b_igate).astype(jnp.float32))
    log_a = LRU_C * r * jax.nn.log_sigmoid(lam.astype(jnp.float32))
    a = jnp.exp(log_a)
    u = jnp.sqrt(-jnp.expm1(2.0 * log_a)) * (i * xc.astype(jnp.float32))
    hs = linear_recurrence(a, u, h0.astype(jnp.float32))
    y = (hs.astype(h.dtype) * jax.nn.gelu(gate)) @ w_out
    return y, hs[:, -1].astype(h.dtype), new_buf

def setup_inputs(seed: int = 0) -> dict:
    key = jax.random.key(seed)
    keys = iter(jax.random.split(key, 80))

    def nrm(shape, scale):
        return jax.random.normal(next(keys), shape, jnp.float32) * scale

    def gain(n):
        return 1.0 + nrm((n,), 0.02)

    def ffn(p):
        return {p + 'norm_ffn': gain(D_MODEL),
                p + 'ffn_w_in': nrm((D_MODEL, 2 * D_FF), D_MODEL ** -0.5),
                p + 'ffn_w_out': nrm((D_FF, D_MODEL), D_FF ** -0.5)}

    def gla(p):
        return {p + 'norm_mix': gain(D_MODEL),
                p + 'gla_w_in': nrm((D_MODEL, GLA_IN), D_MODEL ** -0.5),
                p + 'gla_w_gate_a': nrm((D_MODEL, GLA_GATE_RANK), D_MODEL ** -0.5),
                p + 'gla_w_gate_b': nrm((GLA_GATE_RANK, GLA_HEADS * GLA_DK), GLA_GATE_RANK ** -0.5),
                p + 'gla_b_gate': nrm((GLA_HEADS * GLA_DK,), 0.1),
                p + 'gla_head_norm': gain(GLA_DV),
                p + 'gla_w_out': nrm((GLA_HEADS * GLA_DV, D_MODEL), (GLA_HEADS * GLA_DV) ** -0.5)}

    band_rows = min(ATT_BAND, PAST_LEN)
    inp = {}
    inp['x_prompt'] = nrm((BATCH, SEQ, D_MODEL), 1.0)
    inp['x_sample'] = nrm((DEC_BATCH, DEC_SEQ, D_MODEL), 1.0)
    inp['state_l0_gla'] = nrm((DEC_BATCH, GLA_HEADS, GLA_DK, GLA_DV), 0.5)
    inp['cache_l1_k'] = nrm((DEC_BATCH, band_rows, ATT_HEADS, ATT_DH), 1.0)
    inp['cache_l1_v'] = nrm((DEC_BATCH, band_rows, ATT_HEADS, ATT_DH), 1.0)
    inp['state_l2_h'] = nrm((DEC_BATCH, LRU_WIDTH), 0.5)
    inp['state_l2_conv'] = nrm((DEC_BATCH, CONV_WIDTH - 1, LRU_WIDTH), 1.0)
    inp['state_l3_gla'] = nrm((DEC_BATCH, GLA_HEADS, GLA_DK, GLA_DV), 0.5)
    inp.update(gla('l0_'))
    inp.update(ffn('l0_'))
    inp['l1_norm_mix'] = gain(D_MODEL)
    inp['l1_att_w_qkv'] = nrm((D_MODEL, 3 * D_MODEL), D_MODEL ** -0.5)
    inp['l1_att_rel_bias'] = nrm((ATT_HEADS, 2 * ATT_MAX_REL + 1), 0.2)
    inp['l1_att_w_out'] = nrm((D_MODEL, D_MODEL), D_MODEL ** -0.5)
    inp.update(ffn('l1_'))
    inp['l2_norm_mix'] = gain(D_MODEL)
    inp['l2_lru_w_in'] = nrm((D_MODEL, 2 * LRU_WIDTH), D_MODEL ** -0.5)
    inp['l2_lru_conv_w'] = nrm((CONV_WIDTH, LRU_WIDTH), CONV_WIDTH ** -0.5)
    inp['l2_lru_conv_b'] = nrm((LRU_WIDTH,), 0.02)
    inp['l2_lru_w_rgate'] = nrm((LRU_BLOCKS, LRU_BLOCK, LRU_BLOCK), LRU_BLOCK ** -0.5)
    inp['l2_lru_b_rgate'] = nrm((LRU_WIDTH,), 0.1)
    inp['l2_lru_w_igate'] = nrm((LRU_BLOCKS, LRU_BLOCK, LRU_BLOCK), LRU_BLOCK ** -0.5)
    inp['l2_lru_b_igate'] = nrm((LRU_WIDTH,), 0.1)
    a_c = jax.random.uniform(next(keys), (LRU_WIDTH,), jnp.float32, 0.9, 0.999)
    sig = a_c ** (1.0 / LRU_C)
    inp['l2_lru_lambda'] = jnp.log(sig) - jnp.log1p(-sig)
    inp['l2_lru_w_out'] = nrm((LRU_WIDTH, D_MODEL), LRU_WIDTH ** -0.5)
    inp.update(ffn('l2_'))
    inp.update(gla('l3_'))
    inp.update(ffn('l3_'))
    inp['final_norm'] = gain(D_MODEL)
    return inp

def reference(x_prompt, x_sample, state_l0_gla, cache_l1_k, cache_l1_v, state_l2_h, state_l2_conv, state_l3_gla,
              l0_norm_mix, l0_gla_w_in, l0_gla_w_gate_a, l0_gla_w_gate_b, l0_gla_b_gate, l0_gla_head_norm, l0_gla_w_out,
              l0_norm_ffn, l0_ffn_w_in, l0_ffn_w_out,
              l1_norm_mix, l1_att_w_qkv, l1_att_rel_bias, l1_att_w_out, l1_norm_ffn, l1_ffn_w_in, l1_ffn_w_out,
              l2_norm_mix, l2_lru_w_in, l2_lru_conv_w, l2_lru_conv_b, l2_lru_w_rgate, l2_lru_b_rgate,
              l2_lru_w_igate, l2_lru_b_igate, l2_lru_lambda, l2_lru_w_out, l2_norm_ffn, l2_ffn_w_in, l2_ffn_w_out,
              l3_norm_mix, l3_gla_w_in, l3_gla_w_gate_a, l3_gla_w_gate_b, l3_gla_b_gate, l3_gla_head_norm, l3_gla_w_out,
              l3_norm_ffn, l3_ffn_w_in, l3_ffn_w_out,
              final_norm):
    mix_norms = (l0_norm_mix, l1_norm_mix, l2_norm_mix, l3_norm_mix)
    mix_params = (
        (l0_gla_w_in, l0_gla_w_gate_a, l0_gla_w_gate_b, l0_gla_b_gate, l0_gla_head_norm, l0_gla_w_out),
        (l1_att_w_qkv, l1_att_rel_bias, l1_att_w_out),
        (l2_lru_w_in, l2_lru_conv_w, l2_lru_conv_b, l2_lru_w_rgate, l2_lru_b_rgate,
         l2_lru_w_igate, l2_lru_b_igate, l2_lru_lambda, l2_lru_w_out),
        (l3_gla_w_in, l3_gla_w_gate_a, l3_gla_w_gate_b, l3_gla_b_gate, l3_gla_head_norm, l3_gla_w_out),
    )
    ffn_norms = (l0_norm_ffn, l1_norm_ffn, l2_norm_ffn, l3_norm_ffn)
    ffn_params = ((l0_ffn_w_in, l0_ffn_w_out), (l1_ffn_w_in, l1_ffn_w_out),
                  (l2_ffn_w_in, l2_ffn_w_out), (l3_ffn_w_in, l3_ffn_w_out))
    sample_states = ((state_l0_gla,), (cache_l1_k, cache_l1_v), (state_l2_h, state_l2_conv), (state_l3_gla,))

    xp, xs = x_prompt, x_sample
    Bp = x_prompt.shape[0]
    new_state = []
    for i in range(DEPTH):
        kind = MIXER_PATTERN[i % len(MIXER_PATTERN)]
        hp = rmsnorm(xp, mix_norms[i])
        hs = rmsnorm(xs, mix_norms[i])
        if kind == 'gla':
            s0 = jnp.zeros((Bp, GLA_HEADS, GLA_DK, GLA_DV), xp.dtype)
            yp, sp = gla_mixer(hp, s0, *mix_params[i])
            ys, ss = gla_mixer(hs, *sample_states[i], *mix_params[i])
            new_state.append((sp, ss))
        elif kind == 'band_attn':
            yp, kp_, vp_ = band_attn_prompt(hp, *mix_params[i])
            ys, ks_, vs_ = band_attn_sample(hs, *sample_states[i], *mix_params[i])
            new_state.append((kp_, vp_, ks_, vs_))
        else:
            h0 = jnp.zeros((Bp, LRU_WIDTH), xp.dtype)
            buf0 = jnp.zeros((Bp, CONV_WIDTH - 1, LRU_WIDTH), xp.dtype)
            yp, hlp, bufp = rglru_mixer(hp, h0, buf0, *mix_params[i])
            ys, hls, bufs = rglru_mixer(hs, *sample_states[i], *mix_params[i])
            new_state.append((hlp, bufp, hls, bufs))
        xp = xp + yp
        xs = xs + ys
        xp = xp + swiglu_ffn(rmsnorm(xp, ffn_norms[i]), *ffn_params[i])
        xs = xs + swiglu_ffn(rmsnorm(xs, ffn_norms[i]), *ffn_params[i])

    y_prompt = rmsnorm(xp, final_norm)
    y_sample = rmsnorm(xs, final_norm)
    (gla0_p, gla0_s), (k1_p, v1_p, k1_s, v1_s), (h2_p, conv2_p, h2_s, conv2_s), (gla3_p, gla3_s) = new_state
    return (y_prompt, y_sample, gla0_p, gla0_s, k1_p, v1_p, k1_s, v1_s,
            h2_p, conv2_p, h2_s, conv2_s, gla3_p, gla3_s)


_drawn_inputs = setup_inputs


def setup_inputs(seed=0):
    import zlib

    import numpy as np

    out = dict(_drawn_inputs(seed))
    spreads = {}
    factors = {'l0_gla_head_norm': 2.891,
     'l1_norm_mix': 2.885,
     'l1_norm_ffn': 3.085,
     'l2_norm_mix': 2.751,
     'l2_norm_ffn': 3.943,
     'l3_gla_head_norm': 50.576,
     'l3_norm_ffn': 19.299,
     'final_norm': 27.538,
     'l2_lru_b_rgate': 3.067}
    for name, (base, spread) in spreads.items():
        noise = np.random.default_rng([zlib.crc32(name.encode()), seed]).standard_normal(out[name].shape)
        drawn = base * np.exp(spread * noise) if base else spread * noise
        out[name] = __import__('jax').numpy.asarray(drawn.astype(out[name].dtype))
    for name, factor in factors.items():
        out[name] = (out[name] * factor).astype(out[name].dtype)
    return out
```

```python
from contextlib import ExitStack

import concourse.bass as bass
from concourse import mybir

F32 = mybir.dt.float32
F32R = mybir.dt.float32r
U32 = mybir.dt.uint32
ALU = mybir.AluOpType
ACT = mybir.ActivationFunctionType
AX = mybir.AxisListType
ds = bass.ds

P = 128
D_MODEL, SEQ, DEC_SEQ, PAST = 1024, 512, 32, 256
TOK = SEQ + DEC_SEQ
HALF = TOK // 2
XT = D_MODEL // P
EPS = 1e-6
NEG_INF = -1e30

GLA_HEADS, GLA_DK, GLA_DV, GATE_RANK, GATE_TAU = 4, 128, 256, 16, 16.0
CHUNK = 64
NCHUNK = SEQ // CHUNK
QT = SEQ // P
VT = GLA_DV // P

ATT_HEADS, ATT_DH, MAX_REL = 16, 64, 128
PAIRS = ATT_HEADS // 2
REL = 2 * MAX_REL + 1
BT_ROW = SEQ + P
CT = PAST // P
STEPS = [(e, t) for e in range(2) for t in range(QT + 1)]
LAG = 2
ALL, SAMPLE = slice(0, P), slice(P - DEC_SEQ, P)

LRU_W, LRU_BLK, CONV_W, LRU_C = 1536, 96, 4, 8.0
LT = LRU_W // P
GT = 3
NGROUP = LT // GT
CPAD = CONV_W - 1
GATE_TILES = [[(0, 0), (1, 0)], [(0, 1), (1, 1), (2, 1)], [(1, 2), (2, 2)]]
GATE_LIST = [t for row in GATE_TILES for t in row]

D_FF = 2816
FT = D_FF // P
FH = FT // 2
KMAX = 12

VEC_A = [("l0_norm_mix", XT), ("l0_norm_ffn", XT), ("l1_norm_mix", XT), ("l1_norm_ffn", XT),
         ("l2_norm_mix", XT), ("l2_norm_ffn", XT), ("l3_norm_mix", XT), ("l3_norm_ffn", XT),
         ("final_norm", XT), ("l0_gla_b_gate", 4), ("l3_gla_b_gate", 4),
         ("l0_gla_head_norm", VT), ("l3_gla_head_norm", VT)]
VEC_B = [("l2_lru_conv_b", LT), ("l2_lru_b_rgate", LT), ("l2_lru_b_igate", LT), ("l2_lru_lambda", LT),
         ("state_l2_h", LT), ("l2_lru_conv_w", CONV_W * LT)]
VEC_C = [("state_l2_conv", CPAD * LT)]


def columns(vectors):
    at, out = 0, {}
    for name, n in vectors:
        out[name] = at
        at += n
    return out, at


COL_A, ROWS_A = columns(VEC_A)
COL_B, ROWS_B = columns(VEC_B)
COL_C, ROWS_C = columns(VEC_C)

MIXERS = ["gla", "att", "lru", "gla"]
MIX_BLOCKS = {"gla": 1 + 6 * GLA_HEADS, "att": 3 * PAIRS, "lru": 2 * LT}
MIX_OUT_K = {"gla": XT, "att": XT, "lru": LT}


def schedule(layers):
    at, base = 0, {}
    for i in range(layers):
        for name, n in (("mix_in", MIX_BLOCKS[MIXERS[i]]), ("mix_out", XT),
                        ("up0", 2 * FH), ("down0", XT), ("up1", 2 * FH), ("down1", XT)):
            base[i, name] = at
            at += n
    return base, at


def encoder_step(nc, d, o, layers=4):
    base, total_blocks = schedule(layers)
    stat_of, n_stat = {}, 0
    for i in range(layers):
        stat_of[i, "mix"] = n_stat
        n_stat += 1
        if MIXERS[i] == "gla":
            stat_of[i, "head"] = n_stat
            n_stat += GLA_HEADS
        stat_of[i, "ffn"] = n_stat
        n_stat += 1
    stat_of["final"] = n_stat
    gla_no = {0: 0, 3: 1}
    last = layers - 1

    ctx = ExitStack()
    with ctx:
        def sb(name, shape, dt=F32, c=ctx):
            return c.enter_context(nc.sbuf_tensor(name, shape, dt))

        def sem(name):
            return ctx.enter_context(nc.semaphore(name))

        x = sb("x", [P, XT, TOK])
        xg_hi = sb("xg_hi", [P, XT, TOK], F32R)
        xg_lo = sb("xg_lo", [P, XT, TOK], F32R)
        raw = [sb(f"raw{s}", [P, KMAX, P]) for s in range(2)]
        w_hi = [sb(f"w_hi{s}", [P, KMAX, P], F32R) for s in range(2)]
        w_lo = [sb(f"w_lo{s}", [P, KMAX, P], F32R) for s in range(2)]
        ident = sb("ident", [P, P])
        flip = sb("flip", [P, P])
        mean_x = sb("mean_x", [P, 1])
        mean_v = sb("mean_v", [P, 1])
        eps = sb("eps", [P, 1])
        vec_a = sb("vec_a", [P, ROWS_A])
        vec_b = sb("vec_b", [P, ROWS_B])
        vec_c = sb("vec_c", [P, ROWS_C])
        sq_sum = sb("sq_sum", [P, TOK])
        sq_one = sb("sq_one", [P, TOK])
        rms5 = sb("rms5", [P, QT + 1])
        inv5 = sb("inv5", [P, QT + 1])
        rstd = sb("rstd", [P, TOK])
        chunk_go = sb("chunk_go", [P, TOK])
        tri = sb("tri", [P, P], U32)
        s_in = sb("s_in", [P, GLA_DV])
        lam_t = [sb(f"lam{n}", [P, LT]) for n in range(6)]
        lru_c8 = sb("lru_c8", [P, LT])

        def with_region(make):
            with ExitStack() as c:
                return make(lambda name, shape, dt=F32: sb(name, shape, dt, c))

        def make_start(a):
            return dict(x_rows=a("x_rows", [P, QT + 1, D_MODEL]), vec_rows=a("vec_rows", [P, 3, P]),
                        bias_rows=a("bias_rows", [ATT_HEADS, BT_ROW]), rel_rev=a("rel_rev", [ATT_HEADS, REL - 1]),
                        tri_f=a("tri_f", [P, P]))

        def make_ffn(a):
            return dict(h_hi=a("h_hi", [P, FH, TOK], F32R), h_lo=a("h_lo", [P, FH, TOK], F32R),
                        g=a("ffn_g", [P, TOK]), sg=a("ffn_sg", [P, TOK]), u=a("ffn_u", [P, TOK]))

        def make_gla(a):
            b = {n: a("gla_" + n, [P, TOK]) for n in
                 ("q", "k", "z", "mn", "ez", "b", "eb", "enb", "ekd", "qe", "ke", "kd", "inv")}
            b["oi"], b["yv"] = b["ez"], b["mn"]
            for n in ("v", "r", "o"):
                b[n] = a("gla_" + n, [P, VT, TOK])
            b.update(y_hi=a("gla_y_hi", [P, XT, TOK], F32R), y_lo=a("gla_y_lo", [P, XT, TOK], F32R),
                     low=a("gla_low", [GATE_RANK, TOK]), wb=a("gla_wb", [GATE_RANK, GLA_HEADS * GLA_DK]),
                     wbh=a("gla_wbh", [GATE_RANK, P]), dec=a("gla_dec", [P, NCHUNK + 1]),
                     v_t=a("gla_v_t", [P, QT + 1, GLA_DV]), kd_t=a("gla_kd_t", [P, QT + 1, P]),
                     at=a("gla_at", [P, QT, P]), at_s=a("gla_at_s", [DEC_SEQ, DEC_SEQ]),
                     s=a("gla_s", [P, NCHUNK, GLA_DV]), s_out=a("gla_s_out", [P, GLA_DV]))
            return b

        def make_att(a):
            b = {n: a("att_" + n, [P, TOK]) for n in ("q_rev", "k", "v")}
            b.update(y_hi=a("att_y_hi", [P, XT, TOK], F32R), y_lo=a("att_y_lo", [P, XT, TOK], F32R),
                     k_t=a("att_k_t", [P, QT + 1, P]), v_t=a("att_v_t", [P, QT + 1, P]),
                     kc=a("att_kc", [P, CT, P]), vc=a("att_vc", [P, CT, P]), kc_t=a("att_kc_t", [P, PAST]),
                     bias=a("att_bias", [P, ATT_HEADS, SEQ]),
                     sc=[a(f"att_sc{r}", [P, SEQ]) for r in range(3)],
                     p=[a(f"att_p{r}", [P, SEQ]) for r in range(3)],
                     pt=a("att_pt", [P, QT, SEQ]), pts=a("att_pts", [P, CT + 1, DEC_SEQ]),
                     nmax=a("att_nmax", [P, 3]), tot=a("att_tot", [P, 3]), inv=a("att_inv", [P, 3]))
            return b

        def make_lru(a):
            b = {n: a("lru_" + n, [P, GT, TOK]) for n in ("gate", "xc", "r", "i", "t", "a")}
            b.update(xp=a("lru_xp", [P, GT, CPAD + SEQ + CPAD + DEC_SEQ]),
                     y_hi=a("lru_y_hi", [P, LT, TOK], F32R), y_lo=a("lru_y_lo", [P, LT, TOK], F32R),
                     gate_w=a("lru_gate_w", [P, 2, len(GATE_LIST), P]),
                     tail=a("lru_tail", [P, LT, 8]))
            b["tail_rows"] = b["a"][0:8, :, :].rearrange("p a n -> p (a n)")[:, 0:LRU_W]
            return b

        def make_end(a):
            return dict(y=a("end_y", [P, XT, TOK]), rows=a("end_rows", [P, QT + 1, D_MODEL]))

        ST, FF, GL, AT, LR, EN = (with_region(m) for m in
                                  (make_start, make_ffn, make_gla, make_att, make_lru, make_end))

        slot = [ctx.enter_context(nc.psum_tensor(f"slot{s}", [P, 2, 512], F32)) for s in range(2)]
        A0, A1, A2, A3 = (ctx.enter_context(nc.psum_tensor(f"aux{i}", [P, 512], F32)) for i in range(4))

        def halves(ap):
            return ap.rearrange("p (a n) -> p a n", a=2)

        def one(t, m, cols=slice(0, TOK), rows=slice(0, P)):
            return t[rows, ds(m, 1), cols].rearrange("p a n -> p (a n)")

        bias_dram = nc.dram_tensor("bias_scratch", (ATT_HEADS, BT_ROW), F32).ap()

        s_x, s_vec, s_rel, s_bs = sem("x_rows_in"), sem("vec_rows_in"), sem("rel_in"), sem("bias_stored")
        s_cd, s_cp, s_row = sem("const_vector"), sem("const_pool"), sem("bias_rows")
        s_vt, s_vc = sem("vectors_turned"), sem("vectors_ready")
        s_raw = [sem(f"raw_in{s}") for s in range(2)]
        s_hi, s_lo, s_mm, s_free = sem("w_hi"), sem("w_lo"), sem("block_done"), sem("block_read")
        s_xt, s_x0, s_xhi, s_xlo = sem("x_turned"), sem("x_start"), sem("xg_hi"), sem("xg_lo")
        s_p1, s_p2, s_sq = sem("square"), sem("square_added"), sem("squares_summed")
        s_st1, s_rms, s_inv, s_st2, s_rstd = (sem(n) for n in ("mean_mm", "rms", "inv_rms", "inv_spread", "inv_ready"))
        s_sg, s_h, s_hhi, s_hlo = sem("ffn_silu"), sem("ffn_h"), sem("h_hi"), sem("h_lo")
        s_wb, s_wbh, s_gm, s_z, s_abs, s_exp, s_ln, s_mn, s_g, s_b, s_e, s_df, s_ekd = (sem("gla_" + n) for n in (
            "gate_b_in", "gate_b_head", "gate_mm", "z", "abs", "exp", "ln", "min", "g", "cumsum", "exps", "diff", "exp_kd"))
        s_qe, s_ke, s_kd, s_vtm, s_vte, s_kdm, s_kde, s_atm, s_ate, s_um, s_s, s_om, s_oe, s_sil = (sem("gla_" + n) for n in (
            "qe", "ke", "kd", "v_turned", "v_rows", "kd_turned", "kd_rows", "scores", "masked", "outer", "state",
            "o_mm", "o_read", "silu"))
        s_at0, s_sin, s_sout, s_oi, s_yv, s_yhi, s_ylo = (sem("gla_" + n) for n in (
            "at_zero", "state_in", "state_out", "o_normed", "y", "y_hi", "y_lo"))
        s_bt = [sem("att_bias_in_first"), sem("att_bias_in")]
        s_btm, s_kc, s_tm, s_te, s_kvo, s_sm, s_sc, s_mx, s_p, s_iv, s_pn, s_ptm, s_pte, s_pvm, s_ahi, s_alo = (
            sem("att_" + n) for n in ("bias_masked", "cache_in", "turned", "turned_read", "kv_out", "score_mm",
                                      "score", "neg_max", "prob", "inv_sum", "prob_normed", "prob_turned", "prob_read",
                                      "pv_mm", "y_hi", "y_lo"))
        s_pad, s_gw0, s_gin, s_gelu, s_cst, s_c0, s_tap, s_gsm, s_gmm, s_gsg, s_ta, s_a2, s_w, s_sqr, s_ix, s_u, s_scan = (
            sem("lru_" + n) for n in ("pad", "gate_zero", "gate_in", "gelu", "conv_state", "conv0", "taps", "gate_sample",
                                      "gate_mm", "sigmoid", "tanh_exp", "a2", "w", "sqrt", "ix", "u", "scan"))
        s_lyv, s_lyhi, s_lylo, s_tlm, s_tlr, s_tlo, s_le, s_l = (sem("lru_" + n) for n in (
            "y", "y_hi", "y_lo", "tail_turned", "tail_rows", "tail_out", "lam_exp", "lam"))
        s_yc, s_ym, s_ye0, s_ye1, s_yo, s_lab = (sem(n) for n in ("y_cols", "y_turned", "y_rows_lo", "y_rows_hi", "y_out", "lam_abs"))
        s_go, s_lst, s_p0, s_tri, s_hp = (sem(n) for n in ("go_ones", "lam_steps", "pool_consts", "tri", "head_square"))

        def one3(t, n, a, b, parts=slice(0, P)):
            return t[parts, ds(n, 1), a:b].rearrange("p a n -> p (a n)")

        ORDER = ["mix_in", "mix_out", "up0", "down0", "up1", "down1"]
        END_BANKS = ((A0, A1), (slot[0][:, 0, :], slot[0][:, 1, :]))
        SCORE_RING = (A0, A1, slot[0][:, 0, :])
        GATE_RING = (A0, A1, A3)
        OUTER_RING = (A1, A3, A0)

        def w3(name):
            return d[name].rearrange("(k p) n -> p k n", p=P)

        def gain(name, m):
            return vec_a[:, ds(m + COL_A[name], 1)]

        def norm_after(i, what):
            if what == "mix_out":
                return f"l{i}_norm_ffn"
            return f"l{i + 1}_norm_mix" if i < last else "final_norm"

        def next_k(i, name):
            n = ORDER.index(name) + 1
            if n < len(ORDER):
                return {"mix_out": MIX_OUT_K[MIXERS[i]], "up0": XT, "down0": FH, "up1": XT, "down1": FH}[ORDER[n]]
            if i == last:
                return None
            return "low" if MIXERS[i + 1] == "gla" else XT

        def split_tiles(i, name):
            return XT * (1 + 2 * i + (name == "down1"))

        block = ctx.enter_context(nc.Block())

        @block.sync
        def _(sp):
            for t in range(QT):
                sp.dma_start(ST["x_rows"][:, t, :], d["x_prompt"][0, t * P:(t + 1) * P, :]).then_inc(s_x, 16)
            sp.dma_start(ST["x_rows"][0:DEC_SEQ, QT, :], d["x_sample"][0]).then_inc(s_x, 16)

            def load(b, par, src, kt):
                if not (isinstance(b, int) and b < 2):
                    sp.wait_ge(s_lo, b - 1)
                sp.dma_start(raw[par][:, 0:kt, :], src).then_inc(s_raw[par], 16)

            def load_gates(g):
                if not (isinstance(g, int) and g == 0):
                    sp.wait_ge(s_gmm, g * (2 * GT))
                else:
                    sp.wait_ge(s_gw0, 1)
                for w, name in enumerate(("l2_lru_w_rgate", "l2_lru_w_igate")):
                    for n in range(4):
                        lo, hi = n * LRU_BLK, (n + 1) * LRU_BLK
                        cuts = [lo] + [c for c in (P, 2 * P) if lo < c < hi] + [hi]
                        for r0, r1 in zip(cuts, cuts[1:]):
                            for c0, c1 in zip(cuts, cuts[1:]):
                                at = GATE_LIST.index((r0 // P, c0 // P))
                                src = d[name][ds(g * 4 + n, 1), r0 - lo:r1 - lo, c0 - lo:c1 - lo].rearrange("a r c -> (a r) c")
                                sp.dma_start(LR["gate_w"][r0 % P:r0 % P + r1 - r0, w, at, c0 % P:c0 % P + c1 - c0],
                                             src).then_inc(s_gin, 16)

            for i in range(layers):
                pre, kind = f"l{i}_", MIXERS[i]
                b0 = base[i, "mix_in"]
                if kind == "gla":
                    gl = gla_no[i]
                    w, p0 = w3(pre + "gla_w_in"), b0 % 2
                    if b0:
                        sp.wait_ge(s_lo, b0 - 1)
                    sp.dma_start(raw[p0][:, 0, :].rearrange("p (k n) -> p k n", k=XT),
                                 w3(pre + "gla_w_gate_a")).then_inc(s_raw[p0], 16)

                    def head_blocks(h):
                        cols = [h * P, h * P + GLA_HEADS * GLA_DK] + [
                            h * GLA_DV + (n * D_MODEL + j * P) for n in (1, 2) for j in range(VT)]
                        for j, c in enumerate(cols):
                            load(b0 + 1 + h * 6 + j, (b0 + 1 + j) % 2, w[:, :, ds(c, P)], XT)
                            if j == 3:
                                head_states(h)

                    def head_states(h):
                        if not isinstance(h, int) or h:
                            store_states(h - 1)
                        sp.wait_ge(s_om, h + 4 * gl)
                        sp.dma_start(s_in[:, :], d[f"state_l{i}_gla"][0, ds(h, 1), :, :].rearrange(
                            "a k v -> (a k) v")).then_inc(s_sin, 16)

                    def store_states(h):
                        sp.wait_ge(s_s, (h + (4 * gl + 1)) * (NCHUNK + 1))
                        for n, src in zip((2, 3) if gl == 0 else (12, 13), (GL["s"][:, NCHUNK - 1, :], GL["s_out"][:, :])):
                            sp.dma_start(o[n][0, ds(h, 1), :, :].rearrange("a k v -> (a k) v"), src).then_inc(s_sout, 16)
                    head_blocks(0)
                    with sp.Fori(1, GLA_HEADS) as h:
                        head_blocks(h)
                elif kind == "att":
                    w = w3(pre + "att_w_qkv")

                    def pair_io(j):
                        sp.wait_ge(s_te, j)
                        store_kv(j - 1)
                        sp.wait_ge(s_pvm, j * 2)
                        load_pair(j)

                    def load_pair(j):
                        for dst, name in ((AT["kc"], "cache_l1_k"), (AT["vc"], "cache_l1_v")):
                            src = d[name].rearrange("a (c p) h e -> (a p) c (h e)", p=P)
                            sp.dma_start(dst[:, :, :], src[:, :, ds(j * P, P)]).then_inc(s_kc, 16)

                    def store_kv(j):
                        for n, src in ((4, AT["k_t"]), (5, AT["v_t"])):
                            dst = o[n].rearrange("a (t p) h e -> (a p) t (h e)", p=P)
                            sp.dma_start(dst[:, :, ds(j * P, P)], src[:, 0:QT, :]).then_inc(s_kvo, 16)
                            dst = o[n + 2].rearrange("a t h e -> (a t) (h e)")
                            sp.dma_start(dst[:, ds(j * P, P)], src[0:DEC_SEQ, QT, :]).then_inc(s_kvo, 16)
                    for part in range(3):
                        load(b0 + part, (b0 + part) % 2, w[:, :, part * D_MODEL:part * D_MODEL + P], XT)
                    sp.wait_ge(s_mm, b0 + 1)
                    sp.wait_ge(s_bs, 16)
                    load_pair(0)
                    for h0, h1 in ((0, 2), (2, ATT_HEADS)):
                        src = bass.AP(bias_dram.tensor, h0 * BT_ROW, [[1, P], [BT_ROW, h1 - h0], [1, SEQ]])
                        sp.dma_start(AT["bias"][:, h0:h1, :], src).then_inc(s_bt[h0 > 0], 16)
                    for part in range(3):
                        load(b0 + 3 + part, (b0 + 3 + part) % 2, w[:, :, P + part * D_MODEL:2 * P + part * D_MODEL], XT)
                    pair_io(1)
                    with sp.Fori(1, PAIRS // 2) as jj:
                        for e in range(2):
                            for part in range(3):
                                load(b0 + jj * 6 + (3 * e + part), (b0 + 3 * e + part) % 2,
                                     w[:, :, ds(jj * (2 * P) + (e * P + part * D_MODEL), P)], XT)
                            pair_io(jj * 2 + e)
                else:
                    w = w3(pre + "lru_w_in")

                    def group_blocks(g):
                        for j in range(2 * GT):
                            load(b0 + g * 6 + j, (b0 + j) % 2,
                                 w[:, :, ds(g * (GT * P) + (j // GT * LRU_W + j % GT * P), P)], XT)
                            if j == GT:
                                load_gates(g)
                    group_blocks(0)
                    with sp.Fori(1, NGROUP) as g:
                        group_blocks(g)
                w = w3(pre + {"gla": "gla_w_out", "att": "att_w_out", "lru": "lru_w_out"}[kind])
                b0, kt = base[i, "mix_out"], MIX_OUT_K[kind]
                with sp.Fori(0, XT // 2) as m2:
                    for j in range(2):
                        load(b0 + m2 * 2 + j, (b0 + j) % 2, w[:, :, ds(m2 * (2 * P) + j * P, P)], kt)
                if kind == "gla":
                    store_states(GLA_HEADS - 1)
                elif kind == "att":
                    sp.wait_ge(s_te, PAIRS)
                    store_kv(PAIRS - 1)
                else:
                    sp.wait_ge(s_tlr, GT)
                    for n, rows in ((9, slice(0, 3)), (11, slice(3, 6)), (8, slice(6, 7)), (10, slice(7, 8))):
                        dst = o[n][0] if rows.stop <= 6 else o[n]
                        sp.dma_start(dst, LR["tail_rows"][rows, :]).then_inc(s_tlo, 16)
                wi, wo = w3(pre + "ffn_w_in"), w3(pre + "ffn_w_out")
                for hf in range(2):
                    b0 = base[i, f"up{hf}"]
                    with sp.Fori(0, FH) as t:
                        for j in range(2):
                            load(b0 + t * 2 + j, (b0 + j) % 2, wi[:, :, ds(t * P + (j * D_FF + hf * FH * P), P)], XT)
                    b0 = base[i, f"down{hf}"]
                    with sp.Fori(0, XT // 2) as m2:
                        for j in range(2):
                            load(b0 + m2 * 2 + j, (b0 + j) % 2,
                                 wo[:, hf * FH:(hf + 1) * FH, ds(m2 * (2 * P) + j * P, P)], FH)
            for t in range(QT + 1):
                sp.wait_ge(s_ye0, t + 1)
                sp.wait_ge(s_ye1, t + 1)
                if t < QT:
                    sp.dma_start(o[0][0, t * P:(t + 1) * P, :], EN["rows"][:, t, :]).then_inc(s_yo, 16)
                else:
                    sp.dma_start(o[1][0], EN["rows"][0:DEC_SEQ, t, :]).then_inc(s_yo, 16)
            sp.wait_ge(s_yo, 16 * (QT + 1))

        @block.scalar
        def _(act):
            for v, vectors in enumerate((VEC_A, VEC_B, VEC_C)):
                at = 0
                for name, rows in vectors:
                    src = d[name]
                    form = {1: "(c p) -> c p", 2: "b (c p) -> (b c) p", 3: "a b (c p) -> (a b c) p"}[len(src.shape)]
                    act.dma_start(ST["vec_rows"][at:at + rows, v, :], src.rearrange(form, p=P)).then_inc(s_vec, 16)
                    at += rows

            def split(b, par, kt):
                if kt is None:
                    return
                act.wait_ge(s_raw[par], (b - par) * 8 + 16)
                if not (isinstance(b, int) and b < 2):
                    act.wait_ge(s_mm, b - 1)
                if kt == "low":
                    src = raw[par][:, 0, :].rearrange("p (k n) -> p k n", k=XT)
                    dst = w_hi[par][:, 0:XT, :].rearrange("p k (c n) -> p k c n", n=GATE_RANK)
                    for c in range(P // GATE_RANK):
                        ins = act.activation(dst[:, :, c, :], src, ACT.Copy)
                    ins.then_inc(s_hi, 1)
                else:
                    act.activation(w_hi[par][:, 0:kt, :], raw[par][:, 0:kt, :], ACT.Copy).then_inc(s_hi, 1)

            def xg_split(m, norm):
                act.activation(one(xg_hi, m), one(x, m), ACT.Copy, scale=gain(norm, m)).then_inc(s_xhi, 1)

            def stat(k):
                act.wait_ge(s_st1, k + 1)
                act.activation(rms5[:, 0:QT], A2[:, 480:480 + QT], ACT.Sqrt, bias=eps[:, 0:1])
                act.activation(rms5[0:DEC_SEQ, QT:QT + 1], A2[0:DEC_SEQ, 480 + QT:481 + QT], ACT.Sqrt,
                               bias=eps[0:DEC_SEQ, 0:1]).then_inc(s_rms, 1)

            act.wait_ge(s_vc, 3)
            act.wait_ge(s_cd, 1)
            split(0, 0, "low")
            for m in range(XT):
                act.wait_ge(s_x0, m + 1)
                xg_split(m, "l0_norm_mix")
            lam = vec_b[:, COL_B["l2_lru_lambda"]:COL_B["l2_lru_lambda"] + LT]
            act.activation(lam_t[0][:, :], lam, ACT.Abs).then_inc(s_lab, 1)
            act.wait_ge(s_lab, 1)
            act.activation(lam_t[0][:, :], lam_t[0][:, :], ACT.Exp, scale=-1.0).then_inc(s_le, 1)

            def gla(i, b0):
                gl, k0 = gla_no[i], stat_of[i, "head"]
                par = (b0 + 1) % 2
                split(b0 + 1, par, XT)
                stat(stat_of[i, "mix"])

                def y_split(h, q):
                    for j in range(VT):
                        act.wait_ge(s_yv, q * VT + j + 1)
                        act.activation(one(GL["y_hi"], h * VT + j), GL["yv"][:, :], ACT.Copy).then_inc(s_yhi, 1)

                def head(h, first):
                    b, q = b0 + 1 + h * 6, h + 4 * gl
                    split(b + 1, 1 - par, XT)
                    if not first:
                        stat(h + (k0 - 1))
                        y_split(h - 1, q - 1)
                    split(b + 2, par, XT)
                    act.wait_ge(s_z, q + 1)
                    act.activation(GL["ez"][:, :], GL["z"][:, :], ACT.Abs).then_inc(s_abs, 1)
                    act.wait_ge(s_abs, q + 1)
                    act.activation(GL["ez"][:, :], GL["ez"][:, :], ACT.Exp, scale=-1.0).then_inc(s_exp, 1)
                    act.wait_ge(s_exp, q + 1)
                    act.activation(GL["ez"][:, :], GL["ez"][:, :], ACT.Ln, bias=1.0).then_inc(s_ln, 1)
                    split(b + 3, 1 - par, XT)
                    act.wait_ge(s_b, q + 1)
                    act.wait_ge(s_qe, q)
                    act.wait_ge(s_kd, q)
                    act.wait_ge(s_s, q * (NCHUNK + 1))
                    act.activation(GL["eb"][:, :], GL["b"][:, :], ACT.Exp, scale=1.0 / GATE_TAU)
                    act.activation(GL["enb"][:, :], GL["b"][:, :], ACT.Exp, scale=-1.0 / GATE_TAU)
                    act.activation(GL["dec"][:, 0:NCHUNK], GL["b"][:, CHUNK - 1:SEQ:CHUNK], ACT.Exp, scale=1.0 / GATE_TAU)
                    act.activation(GL["dec"][:, NCHUNK:], GL["b"][:, TOK - 1:TOK], ACT.Exp,
                                   scale=1.0 / GATE_TAU).then_inc(s_e, 1)
                    act.wait_ge(s_df, q + 1)
                    act.activation(GL["ekd"][:, :], GL["z"][:, :], ACT.Exp, scale=1.0 / GATE_TAU).then_inc(s_ekd, 1)
                    split(b + 4, par, XT)
                    act.wait_ge(s_vtm, q + 1)
                    act.wait_ge(s_om, q)
                    for j, bank in enumerate((A0, A1)):
                        act.activation(GL["v_t"][:, 0:QT, j * P:(j + 1) * P],
                                       bank[:, :].rearrange("p (t n) -> p t n", n=P), ACT.Copy)
                    act.activation(GL["v_t"][0:DEC_SEQ, QT, :], A2[0:DEC_SEQ, 64:64 + GLA_DV], ACT.Copy).then_inc(s_vte, 1)
                    split(b + 5, 1 - par, XT)
                    act.wait_ge(s_kdm, q + 1)
                    act.activation(GL["kd_t"][:, 0:QT, :], A3[:, :].rearrange("p (t n) -> p t n", n=P), ACT.Copy)
                    act.activation(GL["kd_t"][0:DEC_SEQ, QT, :], A2[0:DEC_SEQ, 320:320 + P], ACT.Copy).then_inc(s_kde, 1)
                    act.wait_ge(s_free, b + 5)
                    act.activation(GL["r"][:, 0, :], GL["r"][:, 0, :], ACT.Silu).then_inc(s_sil, 1)
                    split(b + 6, par, XT)
                    act.wait_ge(s_free, b + 6)
                    act.activation(GL["r"][:, 1, :], GL["r"][:, 1, :], ACT.Silu).then_inc(s_sil, 1)
                    act.wait_ge(s_om, q + 1)
                    act.activation(GL["o"][:, 0, 0:SEQ], A0[:, :], ACT.Copy)
                    act.activation(GL["o"][:, 1, 0:SEQ], A1[:, :], ACT.Copy)
                    act.activation(GL["o"][:, :, SEQ:TOK], A2[:, 0:VT * DEC_SEQ].rearrange("p (j n) -> p j n", j=VT),
                                   ACT.Copy).then_inc(s_oe, 1)
                head(0, True)
                with act.Fori(1, GLA_HEADS) as h:
                    head(h, False)
                stat(k0 + GLA_HEADS - 1)
                y_split(GLA_HEADS - 1, 4 * gl + GLA_HEADS - 1)

            def attention(i, b0):
                def pair(j, b, par, first, nxt):
                    split(b + 1, 1 - par, XT)
                    if first:
                        stat(stat_of[i, "mix"])
                    split(b + 2, par, XT)
                    split(b + 3, 1 - par, nxt)
                    act.wait_ge(s_tm, j + 1)
                    act.wait_ge(s_pvm, j * 2)
                    act.wait_ge(s_kvo, j * 64)
                    act.activation(AT["k_t"][:, 0:QT, :], A0[:, :].rearrange("p (t n) -> p t n", n=P), ACT.Copy)
                    act.activation(AT["v_t"][:, 0:QT, :], A1[:, :].rearrange("p (t n) -> p t n", n=P), ACT.Copy)
                    act.activation(AT["k_t"][0:DEC_SEQ, QT, :], A2[0:DEC_SEQ, 0:P], ACT.Copy)
                    act.activation(AT["v_t"][0:DEC_SEQ, QT, :], A2[0:DEC_SEQ, P:2 * P], ACT.Copy)
                    act.activation(AT["kc_t"][:, :], A2[:, 2 * P:2 * P + PAST], ACT.Copy).then_inc(s_te, 1)

                    def probs(e, t):
                        z, r = j * 10 + (e * 5 + t), (e * 5 + t) % 3
                        rows, w = (ALL, (t + 1) * P) if t < QT else (SAMPLE, PAST + DEC_SEQ)
                        act.wait_ge(s_mx, z + 1)
                        if e * 5 + t >= 3:
                            act.wait_ge(s_ptm, z - 2)
                        act.activation(AT["p"][r][rows, 0:w], AT["sc"][r][rows, 0:w], ACT.Exp, bias=AT["nmax"][rows, r:r + 1],
                                       accum_out=AT["tot"][rows, r:r + 1]).then_inc(s_p, 1)

                    def cols(e, t):
                        z = j * 10 + (e * 5 + t)
                        act.wait_ge(s_ptm, z + 1)
                        if t == 0:
                            act.wait_ge(s_pvm, j * 2 + e)
                        if t < QT:
                            ins = act.activation(AT["pt"][:, 0:t + 1, t * P:(t + 1) * P],
                                                 A3[:, 0:(t + 1) * P].rearrange("p (k n) -> p k n", n=P), ACT.Copy)
                        else:
                            act.activation(AT["pts"][:, 0:CT, :],
                                           A3[:, 0:CT * DEC_SEQ].rearrange("p (k n) -> p k n", k=CT), ACT.Copy)
                            ins = act.activation(AT["pts"][0:DEC_SEQ, CT, :],
                                                 A3[0:DEC_SEQ, CT * DEC_SEQ:(CT + 1) * DEC_SEQ], ACT.Copy)
                        ins.then_inc(s_pte, 1)

                    def out_hi(e):
                        act.wait_ge(s_pvm, j * 2 + (e + 1))
                        rows = slice(64 * e, 64 * e + 64)
                        act.activation(one(AT["y_hi"], j, slice(0, SEQ), rows), A2[rows, :], ACT.Copy)
                        act.activation(one(AT["y_hi"], j, slice(SEQ, TOK), rows), A3[rows, 480:480 + DEC_SEQ],
                                       ACT.Copy).then_inc(s_ahi, 1)

                    for n, (e, t) in enumerate(STEPS):
                        probs(e, t)
                        if n == LAG + 5:
                            out_hi(0)
                        if n >= LAG:
                            cols(*STEPS[n - LAG])
                    for e, t in STEPS[-LAG:]:
                        cols(e, t)
                    out_hi(1)
                p0 = b0 % 2
                pair(0, b0, p0, True, XT)
                pair(1, b0 + 3, 1 - p0, False, XT)
                with act.Fori(1, PAIRS // 2) as jj:
                    pair(jj * 2, jj * 6 + b0, p0, False, XT)
                    pair(jj * 2 + 1, jj * 6 + (b0 + 3), 1 - p0, False, XT)

            def lru(i, b0):
                def group(g, first, nxt):
                    b, par = g * 6 + b0, b0 % 2
                    for j in range(GT):
                        split(b + j + 1, (par + j + 1) % 2, XT)
                        if first and j == 0:
                            stat(stat_of[i, "mix"])
                        act.wait_ge(s_free, b + j + 1)
                        act.activation(LR["gate"][:, j, :], LR["gate"][:, j, :], ACT.Gelu_apprx_tanh).then_inc(s_gelu, 1)
                    for j in range(GT):
                        split(b + GT + j + 1, (par + GT + j + 1) % 2, XT if j < GT - 1 else nxt)
                        act.wait_ge(s_free, b + (GT + j + 1))
                        act.wait_ge(s_cst, g * GT + (j + 1))
                        cw = vec_b[:, ds(g * GT + (COL_B["l2_lru_conv_w"] + j), 1)]
                        cb = vec_b[:, ds(g * GT + (COL_B["l2_lru_conv_b"] + j), 1)]
                        act.activation(LR["xc"][:, j, 0:SEQ], LR["xp"][:, j, 0:SEQ], ACT.Identity, scale=cw, bias=cb)
                        act.activation(LR["xc"][:, j, SEQ:TOK], LR["xp"][:, j, SEQ + CPAD:TOK + CPAD], ACT.Identity,
                                       scale=cw, bias=cb).then_inc(s_c0, 1)
                    act.wait_ge(s_gsm, g + 1)
                    for n in range(2 * GT):
                        t, dst = n // 2, (LR["r"], LR["i"])[n % 2]
                        name = ("l2_lru_b_rgate", "l2_lru_b_igate")[n % 2]
                        bias = vec_b[:, ds(g * GT + (COL_B[name] + t), 1)]
                        act.wait_ge(s_gmm, g * 6 + (n + 1))
                        act.activation(dst[:, t, SEQ:TOK], A2[:, n * DEC_SEQ:(n + 1) * DEC_SEQ], ACT.Sigmoid, bias=bias)
                        act.activation(dst[:, t, 0:SEQ], GATE_RING[n % 3][:, :], ACT.Sigmoid, bias=bias).then_inc(s_gsg, 1)
                    act.wait_ge(s_gsg, g * 6 + 6)
                    for t in range(GT):
                        c8 = lru_c8[:, ds(g * GT + t, 1)]
                        act.activation(LR["t"][:, t, :], LR["r"][:, t, :], ACT.Tanh, scale=c8)
                        act.activation(LR["a"][:, t, :], LR["r"][:, t, :], ACT.Exp, scale=c8).then_inc(s_ta, 1)
                    for t in range(GT):
                        act.wait_ge(s_w, g * GT + (t + 1))
                        act.activation(LR["t"][:, t, :], LR["r"][:, t, :], ACT.Sqrt, scale=-1.0).then_inc(s_sqr, 1)
                    for t in range(GT):
                        act.wait_ge(s_lyv, g * GT + (t + 1))
                        act.activation(one(LR["y_hi"], g * GT + t), LR["gate"][:, t, :], ACT.Copy).then_inc(s_lyhi, 1)
                act.wait_ge(s_l, 1)
                group(0, True, XT)
                with act.Fori(1, NGROUP - 1) as g:
                    group(g, False, XT)
                group(NGROUP - 1, False, LT)
                for n, bank in enumerate(GATE_RING):
                    act.wait_ge(s_tlm, n + 1)
                    act.activation(LR["tail_rows"][:, n * 512:(n + 1) * 512], bank[0:8, :], ACT.Copy).then_inc(s_tlr, 1)

            def project_out(i, name, b0, kt):
                p0 = b0 % 2
                norm = None if name == "down0" else norm_after(i, name)

                def two(m2, nxt):
                    for j in range(2):
                        split(b0 + m2 * 2 + (j + 1), (p0 + j + 1) % 2, nxt if j else kt)
                        if norm and norm != "final_norm":
                            act.wait_ge(s_free, b0 + m2 * 2 + (j + 1))
                            xg_split(m2 * 2 + j, norm)
                with act.Fori(0, XT // 2 - 1) as m2:
                    two(m2, kt)
                two(XT // 2 - 1, next_k(i, name))

            for i in range(layers):
                {"gla": gla, "att": attention, "lru": lru}[MIXERS[i]](i, base[i, "mix_in"])
                project_out(i, "mix_out", base[i, "mix_out"], MIX_OUT_K[MIXERS[i]])
                for hf in range(2):
                    b0, q0 = base[i, f"up{hf}"], (2 * i + hf) * FH

                    def up(t, first, nxt):
                        split(b0 + t * 2 + 1, 1 - b0 % 2, XT)
                        if first and hf == 0:
                            stat(stat_of[i, "ffn"])
                        act.wait_ge(s_free, b0 + t * 2 + 1)
                        act.activation(FF["sg"][:, :], FF["g"][:, :], ACT.Silu).then_inc(s_sg, 1)
                        split(b0 + t * 2 + 2, b0 % 2, nxt)
                        act.wait_ge(s_h, t + (q0 + 1))
                        act.activation(one(FF["h_hi"], t), FF["u"][:, :], ACT.Copy).then_inc(s_hhi, 1)
                    up(0, True, XT)
                    with act.Fori(1, FH - 1) as t:
                        up(t, False, XT)
                    up(FH - 1, False, FH)
                    project_out(i, f"down{hf}", base[i, f"down{hf}"], FH)
            stat(stat_of["final"])
            for t in range(QT + 1):
                rows = P if t < QT else DEC_SEQ
                act.wait_ge(s_ym, 2 * t + 1)
                act.activation(EN["rows"][0:rows, t, 0:512], END_BANKS[t % 2][0][0:rows, :], ACT.Copy).then_inc(s_ye0, 1)

        @block.vector
        def _(dve):
            dve.memset(mean_x[:, :], 1.0 / D_MODEL)
            dve.memset(mean_v[:, :], 1.0 / GLA_DV)
            dve.memset(chunk_go[:, :], 1.0).then_inc(s_go, 1)
            dve.wait_ge(s_go, 1)
            dve.memset(chunk_go[:, 0:TOK:CHUNK], 0.0)
            dve.memset(eps[:, :], EPS).then_inc(s_cd, 1)
            for v, (dst, rows) in enumerate(((vec_a, ROWS_A), (vec_b, ROWS_B), (vec_c, ROWS_C))):
                if v == 0:
                    dve.wait_ge(s_vt, 3)
                dve.tensor_copy(dst[:, :], A3[:, v * P:v * P + rows]).then_inc(s_vc, 1)

            def split(b, par, kt):
                if kt is None:
                    return
                dve.wait_ge(s_hi, b + 1)
                if kt == "low":
                    src = raw[par][:, 0, :].rearrange("p (k n) -> p k n", k=XT)
                    hi = w_hi[par][:, 0:XT, :].bitcast(F32).rearrange("p k (c n) -> p k c n", n=GATE_RANK)
                    dst = w_lo[par][:, 0:XT, :].rearrange("p k (c n) -> p k c n", n=GATE_RANK)
                    for c in range(P // GATE_RANK):
                        ins = dve.tensor_tensor(dst[:, :, c, :], src, hi[:, :, c, :], ALU.subtract)
                    ins.then_inc(s_lo, 1)
                else:
                    dve.tensor_tensor(w_lo[par][:, 0:kt, :], raw[par][:, 0:kt, :], w_hi[par][:, 0:kt, :].bitcast(F32),
                                      ALU.subtract).then_inc(s_lo, 1)

            def xg_split(m, norm, u):
                dve.wait_ge(s_xhi, u + 1)
                dve.scalar_tensor_tensor(one(xg_lo, m), one(x, m), gain(norm, m), one(xg_hi, m).bitcast(F32),
                                         ALU.mult, ALU.subtract).then_inc(s_xlo, 1)

            def read(b, par, dst, rows=P):
                dve.wait_ge(s_mm, b + 1)
                dve.tensor_tensor(halves(dst), slot[par][0:rows, :, 0:HALF], halves(rstd[0:rows, :]),
                                  ALU.mult).then_inc(s_free, 1)

            def stat(k, dst):
                dve.wait_ge(s_rms, k + 1)
                dve.reciprocal(inv5[:, 0:QT], rms5[:, 0:QT])
                dve.reciprocal(inv5[0:DEC_SEQ, QT:QT + 1], rms5[0:DEC_SEQ, QT:QT + 1]).then_inc(s_inv, 1)
                dve.wait_ge(s_st2, k + 1)
                dve.tensor_copy(dst[:, 0:SEQ], A3[:, :])
                dve.tensor_copy(dst[:, SEQ:TOK], A2[:, 0:DEC_SEQ]).then_inc(s_rstd, 1)
                dve.wait_ge(s_rstd, k + 1)

            split(0, 0, "low")
            for m in range(XT):
                dve.wait_ge(s_xt, m + 1)
                dve.tensor_copy(x[:, m, 0:SEQ], slot[m % 2][:, 0, :])
                dve.tensor_copy(x[:, m, SEQ:TOK], slot[m % 2][:, 1, 0:DEC_SEQ]).then_inc(s_x0, 1)
                xg_split(m, "l0_norm_mix", m)

            e, z, z2, poly, tmp, low = lam_t
            lam = vec_b[:, COL_B["l2_lru_lambda"]:COL_B["l2_lru_lambda"] + LT]
            done = 0

            def step(ins):
                nonlocal done
                done += 1
                ins.then_inc(s_lst, 1)
                dve.wait_ge(s_lst, done)
            dve.wait_ge(s_le, 1)
            step(dve.tensor_scalar(tmp[:, :], e[:, :], 2.0, None, ALU.add))
            step(dve.reciprocal(poly[:, :], tmp[:, :]))
            step(dve.tensor_tensor(z[:, :], e[:, :], poly[:, :], ALU.mult))
            step(dve.tensor_tensor(z2[:, :], z[:, :], z[:, :], ALU.mult))
            step(dve.tensor_scalar(poly[:, :], z2[:, :], 1.0 / 17, 1.0 / 15, ALU.mult, ALU.add))
            for n in (13, 11, 9, 7, 5, 3, 1):
                step(dve.tensor_tensor(tmp[:, :], poly[:, :], z2[:, :], ALU.mult))
                step(dve.tensor_scalar(poly[:, :], tmp[:, :], 1.0 / n, None, ALU.add))
            step(dve.scalar_tensor_tensor(tmp[:, :], poly[:, :], -2.0 * LRU_C, z[:, :], ALU.mult, ALU.mult))
            step(dve.tensor_scalar(low[:, :], lam, 0.0, LRU_C, ALU.min, ALU.mult))
            dve.tensor_tensor(lru_c8[:, :], low[:, :], tmp[:, :], ALU.add).then_inc(s_l, 1)

            def gla(i, b0):
                gl, k0 = gla_no[i], stat_of[i, "head"]
                bg, hn = COL_A[f"l{i}_gla_b_gate"], COL_A[f"l{i}_gla_head_norm"]
                par = (b0 + 1) % 2
                split(b0 + 1, par, XT)
                stat(stat_of[i, "mix"], rstd)
                dve.wait_ge(s_bs, 16)
                dve.memset(GL["at"][:, :, :], 0.0)
                dve.memset(GL["at_s"][:, :], 0.0).then_inc(s_at0, 1)
                read(b0, 1 - par, GL["low"][:, :], GATE_RANK)

                def head_y(h, q):
                    stat(h + k0, GL["inv"])
                    for j in range(VT):
                        n = q * VT + j
                        dve.tensor_tensor(GL["oi"][:, :], GL["o"][:, j, :], GL["inv"][:, :], ALU.mult).then_inc(s_oi, 1)
                        dve.wait_ge(s_oi, n + 1)
                        dve.wait_ge(s_sil, n + 1)
                        dve.scalar_tensor_tensor(GL["yv"][:, :], GL["oi"][:, :], vec_a[:, hn + j:hn + j + 1],
                                                 GL["r"][:, j, :], ALU.mult, ALU.mult).then_inc(s_yv, 1)
                        dve.wait_ge(s_yhi, n + 1)
                        dve.tensor_tensor(one(GL["y_lo"], h * VT + j), GL["yv"][:, :],
                                          one(GL["y_hi"], h * VT + j).bitcast(F32), ALU.subtract).then_inc(s_ylo, 1)

                def head(h, first):
                    b, q = b0 + 1 + h * 6, h + 4 * gl
                    split(b + 1, 1 - par, XT)
                    read(b, par, GL["q"][:, :])
                    if not first:
                        head_y(h - 1, q - 1)
                    split(b + 2, par, XT)
                    dve.wait_ge(s_kd, q)
                    read(b + 1, 1 - par, GL["k"][:, :])
                    dve.wait_ge(s_gm, q + 1)
                    dve.wait_ge(s_ekd, q)
                    bgc = vec_a[:, ds(h + bg, 1)]
                    dve.tensor_scalar(GL["z"][:, 0:SEQ], A0[:, :], bgc, None, ALU.add)
                    dve.tensor_scalar(GL["z"][:, SEQ:TOK], A1[:, 0:DEC_SEQ], bgc, None, ALU.add).then_inc(s_z, 1)
                    dve.wait_ge(s_z, q + 1)
                    dve.tensor_scalar(GL["mn"][:, :], GL["z"][:, :], 0.0, None, ALU.min).then_inc(s_mn, 1)
                    split(b + 3, 1 - par, XT)
                    dve.wait_ge(s_mn, q + 1)
                    dve.wait_ge(s_ln, q + 1)
                    dve.tensor_tensor(GL["mn"][:, :], GL["mn"][:, :], GL["ez"][:, :], ALU.subtract).then_inc(s_g, 1)
                    dve.wait_ge(s_g, q + 1)
                    dve.tensor_tensor_scan(GL["b"][:, :], chunk_go[:, :], GL["mn"][:, :], 0.0, ALU.mult,
                                           ALU.add).then_inc(s_b, 1)
                    dve.wait_ge(s_b, q + 1)
                    dve.tensor_tensor(GL["z"][:, 0:SEQ].rearrange("p (c n) -> p c n", n=CHUNK),
                                      GL["b"][:, CHUNK - 1:SEQ:CHUNK].unsqueeze(2).broadcast_to([P, NCHUNK, CHUNK]),
                                      GL["b"][:, 0:SEQ].rearrange("p (c n) -> p c n", n=CHUNK), ALU.subtract)
                    dve.tensor_tensor(GL["z"][:, SEQ:TOK], GL["b"][:, TOK - 1:TOK].broadcast_to([P, DEC_SEQ]),
                                      GL["b"][:, SEQ:TOK], ALU.subtract).then_inc(s_df, 1)
                    dve.wait_ge(s_vtm, q)
                    read(b + 2, par, GL["v"][:, 0, :])
                    dve.wait_ge(s_e, q + 1)
                    dve.wait_ge(s_om, q)
                    dve.scalar_tensor_tensor(GL["qe"][:, :], GL["q"][:, :], GLA_DK ** -0.5, GL["eb"][:, :],
                                             ALU.mult, ALU.mult).then_inc(s_qe, 1)
                    split(b + 4, par, XT)
                    read(b + 3, 1 - par, GL["v"][:, 1, :])
                    split(b + 5, 1 - par, XT)
                    read(b + 4, par, GL["r"][:, 0, :])
                    split(b + 6, par, XT)
                    dve.wait_ge(s_atm, q + 1)
                    if first:
                        dve.wait_ge(s_at0, gl + 1)
                    read(b + 5, 1 - par, GL["r"][:, 1, :])
                    dve.copy_predicated(GL["at"][:, :, :], tri[:, :].unsqueeze(1).broadcast_to([P, QT, P]),
                                        A0[:, :].rearrange("p (t n) -> p t n", n=P))
                    dve.copy_predicated(GL["at_s"][:, :], tri[0:DEC_SEQ, 0:DEC_SEQ], A2[0:DEC_SEQ, 448:480]).then_inc(s_ate, 1)
                    dve.wait_ge(s_sout, q * 32)
                    for c in range(NCHUNK + 1):
                        n = q * (NCHUNK + 1) + c
                        dve.wait_ge(s_um, n + 1)
                        u = OUTER_RING[c % 3][:, 0:GLA_DV]
                        if c == 0:
                            ins = dve.tensor_copy(GL["s"][:, 0, :], u)
                        else:
                            if c < NCHUNK:
                                dve.wait_ge(s_s, n)
                                src, dst = GL["s"][:, c - 1, :], GL["s"][:, c, :]
                            else:
                                dve.wait_ge(s_sin, q * 16 + 16)
                                src, dst = s_in[:, :], GL["s_out"][:, :]
                            ins = dve.scalar_tensor_tensor(dst, src, GL["dec"][:, c:c + 1], u, ALU.mult, ALU.add)
                        ins.then_inc(s_s, 1)
                head(0, True)
                with dve.Fori(1, GLA_HEADS) as h:
                    head(h, False)
                head_y(GLA_HEADS - 1, 4 * gl + GLA_HEADS - 1)

            def attention(i, b0):
                def pair(j, b, par, first, nxt):
                    split(b + 1, 1 - par, XT)
                    if first:
                        stat(stat_of[i, "mix"], rstd)
                    dve.wait_ge(s_sm, j * 10)
                    read(b, par, AT["q_rev"][:, ::-1])
                    split(b + 2, par, XT)
                    read(b + 1, 1 - par, AT["k"][:, :])
                    split(b + 3, 1 - par, nxt)
                    read(b + 2, par, AT["v"][:, :])

                    def scores(e, t):
                        z, r = j * 10 + (e * 5 + t), (e * 5 + t) % 3
                        rows, w = (ALL, (t + 1) * P) if t < QT else (SAMPLE, PAST + DEC_SEQ)
                        at = SEQ - w if t < QT else P
                        dve.wait_ge(s_sm, z + 1)
                        if t == 0 and isinstance(j, int):
                            dve.wait_ge(s_btm, j + 1)
                        if e * 5 + t >= 3:
                            dve.wait_ge(s_p, z - 2)
                        dve.scalar_tensor_tensor(AT["sc"][r][rows, 0:w], SCORE_RING[r][rows, 0:w], ATT_DH ** -0.5,
                                                 one3(AT["bias"], j * 2 + e, at, at + w, rows), ALU.mult, ALU.add).then_inc(s_sc, 1)
                        dve.wait_ge(s_sc, z + 1)
                        dve.tensor_reduce(AT["nmax"][rows, r:r + 1], AT["sc"][r][rows, 0:w], AX.X, ALU.max,
                                          negate=True).then_inc(s_mx, 1)

                    def inverse(e, t):
                        z, r = j * 10 + (e * 5 + t), (e * 5 + t) % 3
                        rows = ALL if t < QT else SAMPLE
                        dve.wait_ge(s_p, z + 1)
                        dve.reciprocal(AT["inv"][rows, r:r + 1], AT["tot"][rows, r:r + 1]).then_inc(s_iv, 1)
                        dve.wait_ge(s_iv, z + 1)
                        w = (t + 1) * P if t < QT else PAST + DEC_SEQ
                        dve.tensor_tensor(AT["p"][r][rows, 0:w], AT["p"][r][rows, 0:w],
                                          AT["inv"][rows, r:r + 1].broadcast_to([rows.stop - rows.start, w]),
                                          ALU.mult).then_inc(s_pn, 1)

                    def out_lo(e):
                        dve.wait_ge(s_ahi, j * 2 + (e + 1))
                        rows = slice(64 * e, 64 * e + 64)
                        for bank, cols in ((A2[rows, :], slice(0, SEQ)), (A3[rows, 480:480 + DEC_SEQ], slice(SEQ, TOK))):
                            ins = dve.tensor_tensor(one(AT["y_lo"], j, cols, rows), bank,
                                                    one(AT["y_hi"], j, cols, rows).bitcast(F32), ALU.subtract)
                        ins.then_inc(s_alo, 1)

                    for n, (e, t) in enumerate(STEPS):
                        scores(e, t)
                        if n:
                            inverse(*STEPS[n - 1])
                        if n == LAG + 5:
                            out_lo(0)
                    inverse(*STEPS[-1])
                    out_lo(1)
                p0 = b0 % 2
                pair(0, b0, p0, True, XT)
                pair(1, b0 + 3, 1 - p0, False, XT)
                with dve.Fori(1, PAIRS // 2) as jj:
                    pair(jj * 2, jj * 6 + b0, p0, False, XT)
                    pair(jj * 2 + 1, jj * 6 + (b0 + 3), 1 - p0, False, XT)

            def lru(i, b0):
                conv_state = vec_c[:, :].rearrange("p (r c) -> p r c", c=LT)

                def group(g, first, nxt):
                    b, par = g * 6 + b0, b0 % 2
                    for j in range(GT):
                        split(b + j + 1, (par + j + 1) % 2, XT)
                        if first and j == 0:
                            stat(stat_of[i, "mix"], rstd)
                            dve.memset(LR["xp"][:, :, 0:CPAD], 0.0).then_inc(s_pad, 1)
                            dve.wait_ge(s_pad, 1)
                        read(b + j, (par + j) % 2, LR["gate"][:, j, :])
                    for j in range(GT):
                        split(b + GT + j + 1, (par + GT + j + 1) % 2, XT if j < GT - 1 else nxt)
                        n, ps = g * GT + j, slot[(par + GT + j) % 2]
                        dve.tensor_copy(LR["xp"][:, j, CPAD + SEQ:CPAD + SEQ + CPAD].unsqueeze(2),
                                        conv_state[:, :, ds(n, 1)]).then_inc(s_cst, 1)
                        dve.wait_ge(s_mm, b + (GT + j + 1))
                        cut = SEQ - HALF
                        dve.tensor_tensor(LR["xp"][:, j, CPAD:CPAD + HALF], ps[:, 0, 0:HALF], rstd[:, 0:HALF], ALU.mult)
                        dve.tensor_tensor(LR["xp"][:, j, CPAD + HALF:CPAD + SEQ], ps[:, 1, 0:cut], rstd[:, HALF:SEQ], ALU.mult)
                        dve.tensor_tensor(LR["xp"][:, j, 2 * CPAD + SEQ:], ps[:, 1, cut:HALF], rstd[:, SEQ:TOK],
                                          ALU.mult).then_inc(s_free, 1)
                        dve.wait_ge(s_c0, n + 1)
                        for tap in range(1, CONV_W):
                            cw = vec_b[:, ds(n + (COL_B["l2_lru_conv_w"] + tap * LT), 1)]
                            for at, cols in ((tap, slice(0, SEQ)), (SEQ + CPAD + tap, slice(SEQ, TOK))):
                                ins = dve.scalar_tensor_tensor(LR["xc"][:, j, cols], LR["xp"][:, j, at:at + cols.stop - cols.start],
                                                               cw, LR["xc"][:, j, cols], ALU.mult, ALU.add)
                            ins.then_inc(s_tap, 1)
                            dve.wait_ge(s_tap, n * 3 + tap)
                        dve.tensor_copy(one3(LR["tail"], n, 0, 3), LR["xp"][:, j, SEQ:SEQ + CPAD])
                        dve.tensor_copy(one3(LR["tail"], n, 3, 6), LR["xp"][:, j, TOK + CPAD:TOK + 2 * CPAD])
                    for t in range(GT):
                        dve.wait_ge(s_gsg, g * 6 + (2 * t + 2))
                        dve.tensor_tensor(LR["i"][:, t, :], LR["i"][:, t, :], LR["xc"][:, t, :], ALU.mult).then_inc(s_ix, 1)
                    for t in range(GT):
                        dve.wait_ge(s_ta, g * GT + (t + 1))
                        dve.tensor_tensor(LR["r"][:, t, :], LR["a"][:, t, :], LR["a"][:, t, :], ALU.mult).then_inc(s_a2, 1)
                        dve.wait_ge(s_a2, g * GT + (t + 1))
                        dve.scalar_tensor_tensor(LR["r"][:, t, :], LR["r"][:, t, :], 1.0, LR["t"][:, t, :],
                                                 ALU.add, ALU.mult).then_inc(s_w, 1)
                    for t in range(GT):
                        n = g * GT + t
                        dve.wait_ge(s_sqr, n + 1)
                        dve.wait_ge(s_ix, n + 1)
                        dve.tensor_tensor(LR["i"][:, t, :], LR["i"][:, t, :], LR["t"][:, t, :], ALU.mult).then_inc(s_u, 1)
                        dve.wait_ge(s_u, n + 1)
                        dve.tensor_tensor_scan(LR["xc"][:, t, 0:SEQ], LR["a"][:, t, 0:SEQ], LR["i"][:, t, 0:SEQ], 0.0,
                                               ALU.mult, ALU.add)
                        dve.tensor_tensor_scan(LR["xc"][:, t, SEQ:TOK], LR["a"][:, t, SEQ:TOK], LR["i"][:, t, SEQ:TOK],
                                               vec_b[:, ds(n + COL_B["state_l2_h"], 1)], ALU.mult, ALU.add).then_inc(s_scan, 1)
                        dve.wait_ge(s_scan, n + 1)
                        dve.tensor_copy(one3(LR["tail"], n, 6, 7), LR["xc"][:, t, SEQ - 1:SEQ])
                        dve.tensor_copy(one3(LR["tail"], n, 7, 8), LR["xc"][:, t, TOK - 1:TOK])
                        dve.wait_ge(s_gelu, n + 1)
                        dve.tensor_tensor(LR["gate"][:, t, :], LR["xc"][:, t, :], LR["gate"][:, t, :], ALU.mult).then_inc(s_lyv, 1)
                        dve.wait_ge(s_lyv, n + 1)
                        dve.wait_ge(s_lyhi, n + 1)
                        dve.tensor_tensor(one(LR["y_lo"], n), LR["gate"][:, t, :], one(LR["y_hi"], n).bitcast(F32),
                                          ALU.subtract).then_inc(s_lylo, 1)
                group(0, True, XT)
                with dve.Fori(1, NGROUP - 1) as g:
                    group(g, False, XT)
                group(NGROUP - 1, False, LT)

            def project_out(i, name, b0, kt):
                p0 = b0 % 2
                norm = None if name == "down0" else norm_after(i, name)

                def two(m2, nxt):
                    for j in range(2):
                        m, b = m2 * 2 + j, b0 + m2 * 2 + j
                        split(b + 1, (p0 + j + 1) % 2, nxt if j else kt)
                        dve.wait_ge(s_mm, b + 1)
                        dve.tensor_tensor(halves(one(x, m)), slot[(p0 + j) % 2][:, :, 0:HALF], halves(one(x, m)),
                                          ALU.add).then_inc(s_free, 1)
                        if norm and norm != "final_norm":
                            xg_split(m, norm, m + split_tiles(i, name))
                with dve.Fori(0, XT // 2 - 1) as m2:
                    two(m2, kt)
                two(XT // 2 - 1, next_k(i, name))

            for i in range(layers):
                {"gla": gla, "att": attention, "lru": lru}[MIXERS[i]](i, base[i, "mix_in"])
                project_out(i, "mix_out", base[i, "mix_out"], MIX_OUT_K[MIXERS[i]])
                for hf in range(2):
                    b0, q0 = base[i, f"up{hf}"], (2 * i + hf) * FH

                    def up(t, first, nxt):
                        b, p0 = b0 + t * 2, b0 % 2
                        split(b + 1, 1 - p0, XT)
                        if first and hf == 0:
                            stat(stat_of[i, "ffn"], rstd)
                        read(b, p0, FF["g"][:, :])
                        split(b + 2, p0, nxt)
                        read(b + 1, 1 - p0, FF["u"][:, :])
                        dve.wait_ge(s_free, b + 2)
                        dve.wait_ge(s_sg, t + (q0 + 1))
                        dve.tensor_tensor(FF["u"][:, :], FF["sg"][:, :], FF["u"][:, :], ALU.mult).then_inc(s_h, 1)
                        dve.wait_ge(s_hhi, t + (q0 + 1))
                        dve.tensor_tensor(one(FF["h_lo"], t), FF["u"][:, :], one(FF["h_hi"], t).bitcast(F32),
                                          ALU.subtract).then_inc(s_hlo, 1)
                    up(0, True, XT)
                    with dve.Fori(1, FH - 1) as t:
                        up(t, False, XT)
                    up(FH - 1, False, FH)
                    project_out(i, f"down{hf}", base[i, f"down{hf}"], FH)
            stat(stat_of["final"], rstd)
            for m in range(XT):
                dve.scalar_tensor_tensor(EN["y"][:, m, :], x[:, m, :], gain("final_norm", m), rstd[:, :],
                                         ALU.mult, ALU.mult).then_inc(s_yc, 1)
            for t in range(QT + 1):
                rows = P if t < QT else DEC_SEQ
                dve.wait_ge(s_ym, 2 * t + 2)
                dve.tensor_copy(EN["rows"][0:rows, t, 512:1024], END_BANKS[t % 2][1][0:rows, :]).then_inc(s_ye1, 1)

        @block.tensor
        def _(pe):
            def turn(out, in_):
                return pe.matmul(out, in_, ident[0:in_.shape[0], 0:in_.shape[0]], start=True, stop=True)

            def turn_flip(out, in_, back):
                return pe.matmul(out, in_, back, start=True, stop=True)

            pe.wait_ge(s_cp, 2)
            n_vec = len(VEC_A) + len(VEC_B) + len(VEC_C)
            pe.wait_ge(s_vec, 16 * n_vec)
            for v, rows in enumerate((ROWS_A, ROWS_B, ROWS_C)):
                turn(A3[:, v * P:v * P + rows], ST["vec_rows"][0:rows, v, :]).then_inc(s_vt, 1)
            pe.wait_ge(s_x, 16 * (QT + 1))
            for m in range(XT):
                if m >= 2:
                    pe.wait_ge(s_x0, m - 1)
                for t in range(QT):
                    turn(slot[m % 2][:, 0, t * P:(t + 1) * P], ST["x_rows"][:, t, m * P:(m + 1) * P])
                turn(slot[m % 2][:, 1, 0:DEC_SEQ], ST["x_rows"][0:DEC_SEQ, QT, m * P:(m + 1) * P]).then_inc(s_xt, 1)
            pe.wait_ge(s_x0, XT)

            def mm_block(b, par, kt, hi, lo, ready=None, hooks={}):
                pe.wait_ge(s_lo, b + 1)
                if not (isinstance(b, int) and b < 2):
                    pe.wait_ge(s_free, b - 1)
                for k in range(kt):
                    if k in hooks:
                        hooks[k]()
                    if ready:
                        pe.wait_ge(ready[0], ready[1](k))
                    for w, a, at in ((w_hi, hi, 0), (w_hi, lo, 1), (w_lo, hi, 2)):
                        for hf in range(2):
                            ins = pe.matmul(slot[par][:, hf, 0:HALF], w[par][:, k, :], a[:, k, hf * HALF:(hf + 1) * HALF],
                                            start=(k == 0 and at == 0), stop=(k == kt - 1 and at == 2))
                ins.then_inc(s_mm, 1)

            def stat_sum(k, mean):
                pe.wait_ge(s_sq, k + 1)
                for t in range(QT):
                    pe.matmul(A2[:, 480 + t:481 + t], sq_sum[:, t * P:(t + 1) * P], mean[:, 0:1], start=True, stop=True)
                pe.matmul(A2[0:DEC_SEQ, 480 + QT:481 + QT], sq_sum[:, SEQ:TOK], mean[:, 0:1], start=True,
                          stop=True).then_inc(s_st1, 1)

            def stat_spread(k):
                pe.wait_ge(s_inv, k + 1)
                for t in range(QT):
                    pe.matmul(A3[:, t * P:(t + 1) * P], inv5[:, t:t + 1].broadcast_to([P, P]), ident[:, :], start=True, stop=True)
                pe.matmul(A2[:, 0:DEC_SEQ], inv5[0:DEC_SEQ, QT:QT + 1].broadcast_to([DEC_SEQ, P]),
                          ident[0:DEC_SEQ, 0:DEC_SEQ], start=True, stop=True).then_inc(s_st2, 1)

            def first_two(i, b0, k, seen, extra=None):
                p0 = b0 % 2
                mm_block(b0, p0, XT, xg_hi, xg_lo, ready=(s_xlo, lambda n: seen + n + 1))
                stat_sum(k, mean_x)
                mm_block(b0 + 1, 1 - p0, XT, xg_hi, xg_lo, hooks={4: lambda: stat_spread(k)})

            def gla(i, b0):
                gl, k0 = gla_no[i], stat_of[i, "head"]
                par = (b0 + 1) % 2
                first_two(i, b0, stat_of[i, "mix"], XT * 2 * i)

                def head(h, first):
                    b, q = b0 + 1 + h * 6, h + 4 * gl
                    if not first:
                        mm_block(b, par, XT, xg_hi, xg_lo)
                        stat_sum(h + (k0 - 1), mean_v)
                        mm_block(b + 1, 1 - par, XT, xg_hi, xg_lo, hooks={4: lambda: stat_spread(h + (k0 - 1))})
                    else:
                        mm_block(b + 1, 1 - par, XT, xg_hi, xg_lo)
                        pe.wait_ge(s_free, b0 + 1)
                        pe.wait_ge(s_rstd, stat_of[i, "mix"] + 1)
                    pe.wait_ge(s_wbh, q + 1)
                    pe.wait_ge(s_oe, q)
                    pe.matmul(A0[:, :], GL["wbh"][:, :], GL["low"][:, 0:SEQ], start=True, stop=True)
                    pe.matmul(A1[:, 0:DEC_SEQ], GL["wbh"][:, :], GL["low"][:, SEQ:TOK], start=True, stop=True).then_inc(s_gm, 1)
                    mm_block(b + 2, par, XT, xg_hi, xg_lo)
                    mm_block(b + 3, 1 - par, XT, xg_hi, xg_lo)
                    pe.wait_ge(s_free, b + 4)
                    pe.wait_ge(s_z, q + 1)
                    if not first:
                        pe.wait_ge(s_rstd, h + k0)
                    for j, bank in enumerate((A0, A1)):
                        for t in range(QT):
                            turn(bank[:, t * P:(t + 1) * P], GL["v"][:, j, t * P:(t + 1) * P])
                    for j in range(VT):
                        ins = turn(A2[0:DEC_SEQ, 64 + j * P:64 + (j + 1) * P], GL["v"][:, j, SEQ:TOK])
                    ins.then_inc(s_vtm, 1)
                    mm_block(b + 4, par, XT, xg_hi, xg_lo)
                    pe.wait_ge(s_kd, q + 1)
                    pe.wait_ge(s_vte, q + 1)
                    for t in range(QT):
                        turn(A3[:, t * P:(t + 1) * P], GL["kd"][:, t * P:(t + 1) * P])
                    turn(A2[0:DEC_SEQ, 320:320 + P], GL["kd"][:, SEQ:TOK]).then_inc(s_kdm, 1)
                    mm_block(b + 5, 1 - par, XT, xg_hi, xg_lo)
                    pe.wait_ge(s_qe, q + 1)
                    pe.wait_ge(s_ke, q + 1)
                    pe.wait_ge(s_kde, q + 1)
                    for t in range(QT):
                        cols = slice(t * P, (t + 1) * P)
                        pe.matmul(A0[:, cols], GL["ke"][:, cols], GL["qe"][:, cols], start=True, stop=True)
                    pe.matmul(A2[0:DEC_SEQ, 448:480], GL["ke"][:, SEQ:TOK], GL["qe"][:, SEQ:TOK], start=True,
                              stop=True).then_inc(s_atm, 1)
                    for c in range(NCHUNK + 1):
                        rows = slice(c % 2 * CHUNK, c % 2 * CHUNK + (CHUNK if c < NCHUNK else DEC_SEQ))
                        if c == 2:
                            pe.wait_ge(s_ate, q + 1)
                        if c >= 3:
                            pe.wait_ge(s_s, q * (NCHUNK + 1) + (c - 2))
                        pe.matmul(OUTER_RING[c % 3][:, 0:GLA_DV],
                                  GL["kd_t"][rows, c // 2, :], GL["v_t"][rows, c // 2, :], start=True, stop=True).then_inc(s_um, 1)
                    pe.wait_ge(s_s, q * (NCHUNK + 1) + (NCHUNK + 1))
                    for j, bank in enumerate((A0, A1)):
                        vj = slice(j * P, (j + 1) * P)
                        for t in range(QT):
                            pe.matmul(bank[:, t * P:(t + 1) * P], GL["v_t"][:, t, vj], GL["at"][:, t, :], start=True, stop=False)
                            for c in (2 * t, 2 * t + 1):
                                if c:
                                    cols = slice(c * CHUNK, (c + 1) * CHUNK)
                                    pe.matmul(bank[:, cols], GL["s"][:, c - 1, vj], GL["qe"][:, cols], start=False, stop=bool(c % 2))
                        out = A2[:, j * DEC_SEQ:(j + 1) * DEC_SEQ]
                        pe.matmul(out, GL["v_t"][0:DEC_SEQ, QT, vj], GL["at_s"][:, :], start=True, stop=False)
                        ins = pe.matmul(out, s_in[:, vj], GL["qe"][:, SEQ:TOK], start=False, stop=True)
                    ins.then_inc(s_om, 1)
                head(0, True)
                with pe.Fori(1, GLA_HEADS) as h:
                    head(h, False)
                stat_after = k0 + GLA_HEADS - 1
                stat_sum(stat_after, mean_v)
                stat_spread(stat_after)
                return GL["y_hi"], GL["y_lo"], (s_ylo, lambda n: gl * XT + n + 1)

            def attention(i, b0):
                def pair(j, b, par, first):
                    if first:
                        first_two(i, b, stat_of[i, "mix"], XT * 2 * i)
                    else:
                        mm_block(b, par, XT, xg_hi, xg_lo)
                        mm_block(b + 1, 1 - par, XT, xg_hi, xg_lo)
                    mm_block(b + 2, par, XT, xg_hi, xg_lo)
                    pe.wait_ge(s_free, b + 3)
                    pe.wait_ge(s_kc, j * 32 + 32)
                    pe.wait_ge(s_alo, j * 2)
                    for t in range(QT):
                        turn(A0[:, t * P:(t + 1) * P], AT["k"][:, t * P:(t + 1) * P])
                        turn(A1[:, t * P:(t + 1) * P], AT["v"][:, t * P:(t + 1) * P])
                    turn(A2[0:DEC_SEQ, 0:P], AT["k"][:, SEQ:TOK])
                    turn(A2[0:DEC_SEQ, P:2 * P], AT["v"][:, SEQ:TOK])
                    for c in range(CT):
                        ins = turn(A2[:, (2 + c) * P:(3 + c) * P], AT["kc"][:, c, :])
                    ins.then_inc(s_tm, 1)
                    pe.wait_ge(s_te, j + 1)

                    def scores(e, t):
                        r, rows = (e * 5 + t) % 3, slice(64 * e, 64 * e + 64)
                        bank = SCORE_RING[r]
                        if t < QT:
                            ins = pe.matmul(bank[:, 0:(t + 1) * P], AT["q_rev"][rows, TOK - (t + 1) * P:TOK - t * P],
                                            AT["k"][rows, 0:(t + 1) * P], start=True, stop=True)
                        else:
                            pe.matmul(bank[SAMPLE, 0:PAST], AT["q_rev"][rows, 0:DEC_SEQ], AT["kc_t"][rows, :], start=True, stop=True)
                            ins = pe.matmul(bank[SAMPLE, PAST:PAST + DEC_SEQ], AT["q_rev"][rows, 0:DEC_SEQ],
                                            AT["k"][rows, SEQ:TOK], start=True, stop=True)
                        ins.then_inc(s_sm, 1)

                    def turn_p(e, t):
                        z = j * 10 + (e * 5 + t)
                        pr = AT["p"][(e * 5 + t) % 3]
                        pe.wait_ge(s_pn, z + 1)
                        pe.wait_ge(s_pte, z)
                        if t == 0:
                            pe.wait_ge(s_alo, j * 2 + e)
                        if t < QT:
                            for k in range(t + 1):
                                ins = turn_flip(A3[:, k * P:(k + 1) * P], pr[:, k * P:(k + 1) * P], flip[:, :])
                        else:
                            for k in range(CT):
                                turn_flip(A3[:, k * DEC_SEQ:(k + 1) * DEC_SEQ], pr[SAMPLE, k * P:(k + 1) * P], flip[SAMPLE, 0:DEC_SEQ])
                            ins = turn_flip(A3[0:DEC_SEQ, CT * DEC_SEQ:(CT + 1) * DEC_SEQ], pr[SAMPLE, PAST:PAST + DEC_SEQ],
                                            flip[SAMPLE, 0:DEC_SEQ])
                        ins.then_inc(s_ptm, 1)

                    def weigh(e):
                        pe.wait_ge(s_pte, j * 10 + (e * 5 + 5))
                        pe.wait_ge(s_alo, j * 2 + e)
                        rows = slice(64 * e, 64 * e + 64)
                        for k in range(QT):
                            pe.matmul(A2[rows, k * P:SEQ], AT["v_t"][:, k, rows], AT["pt"][:, k, k * P:SEQ],
                                      start=(k == 0), stop=(k == QT - 1))
                        out = A3[rows, 480:480 + DEC_SEQ]
                        for k in range(CT):
                            pe.matmul(out, AT["vc"][:, k, rows], AT["pts"][:, k, :], start=(k == 0), stop=False)
                        pe.matmul(out, AT["v_t"][0:DEC_SEQ, QT, rows], AT["pts"][0:DEC_SEQ, CT, :], start=False,
                                  stop=True).then_inc(s_pvm, 1)

                    for n, (e, t) in enumerate(STEPS):
                        scores(e, t)
                        if n == LAG + 5:
                            weigh(0)
                        if n >= LAG:
                            turn_p(*STEPS[n - LAG])
                    for e, t in STEPS[-LAG:]:
                        turn_p(e, t)
                    weigh(1)
                p0 = b0 % 2
                pair(0, b0, p0, True)
                pair(1, b0 + 3, 1 - p0, False)
                with pe.Fori(1, PAIRS // 2) as jj:
                    pair(jj * 2, jj * 6 + b0, p0, False)
                    pair(jj * 2 + 1, jj * 6 + (b0 + 3), 1 - p0, False)
                return AT["y_hi"], AT["y_lo"], (s_alo, lambda n: 2 * n + 2)

            def lru(i, b0):
                def group(g, first):
                    b, par = g * 6 + b0, b0 % 2
                    if first:
                        first_two(i, b, stat_of[i, "mix"], XT * 2 * i)
                    for j in range(2 if first else 0, 2 * GT):
                        mm_block(b + j, (par + j) % 2, XT, xg_hi, xg_lo)
                    pe.wait_ge(s_tap, g * 9 + 9)
                    pe.wait_ge(s_gin, g * (20 * 16) + 20 * 16)
                    if first:
                        pe.wait_ge(s_rstd, stat_of[i, "mix"] + 1)
                    pe.wait_ge(s_gsg, g * 6)

                    def gate(out, w, t, cols):
                        for n, (k, _) in enumerate(GATE_TILES[t]):
                            ins = pe.matmul(out, LR["gate_w"][:, w, GATE_LIST.index((k, t)), :], LR["xc"][:, k, cols],
                                            start=(n == 0), stop=(n == len(GATE_TILES[t]) - 1))
                        return ins
                    for n in range(2 * GT):
                        ins = gate(A2[:, n * DEC_SEQ:(n + 1) * DEC_SEQ], n % 2, n // 2, slice(SEQ, TOK))
                    ins.then_inc(s_gsm, 1)
                    for n in range(2 * GT):
                        if n >= 3:
                            pe.wait_ge(s_gsg, g * 6 + (n - 2))
                        gate(GATE_RING[n % 3][:, :], n % 2, n // 2, slice(0, SEQ)).then_inc(s_gmm, 1)
                group(0, True)
                with pe.Fori(1, NGROUP) as g:
                    group(g, False)
                pe.wait_ge(s_gsg, 6 * NGROUP)
                pe.wait_ge(s_lylo, LT)
                for n, bank in enumerate(GATE_RING):
                    for c in range(4):
                        ins = turn(bank[0:8, c * P:(c + 1) * P], LR["tail"][:, 4 * n + c, :])
                    ins.then_inc(s_tlm, 1)
                return LR["y_hi"], LR["y_lo"], (s_lylo, lambda n: n + 1)

            def project_out(b0, kt, hi, lo, ready):
                p0 = b0 % 2
                mm_block(b0, p0, kt, hi, lo, ready=ready)
                mm_block(b0 + 1, 1 - p0, kt, hi, lo)
                with pe.Fori(1, XT // 2) as m2:
                    mm_block(b0 + m2 * 2, p0, kt, hi, lo)
                    mm_block(b0 + m2 * 2 + 1, 1 - p0, kt, hi, lo)

            for i in range(layers):
                hi, lo, ready = {"gla": gla, "att": attention, "lru": lru}[MIXERS[i]](i, base[i, "mix_in"])
                project_out(base[i, "mix_out"], MIX_OUT_K[MIXERS[i]], hi, lo, ready)
                for hf in range(2):
                    b0 = base[i, f"up{hf}"]
                    if hf == 0:
                        first_two(i, b0, stat_of[i, "ffn"], XT * (2 * i + 1))
                    with pe.Fori(1 if hf == 0 else 0, FH) as t:
                        mm_block(b0 + t * 2, b0 % 2, XT, xg_hi, xg_lo)
                        mm_block(b0 + t * 2 + 1, 1 - b0 % 2, XT, xg_hi, xg_lo)
                    q0 = (2 * i + hf) * FH
                    project_out(base[i, f"down{hf}"], FH, FF["h_hi"], FF["h_lo"], (s_hlo, lambda n: q0 + n + 1))
            stat_sum(stat_of["final"], mean_x)
            stat_spread(stat_of["final"])
            pe.wait_ge(s_yc, XT)
            pe.wait_ge(s_free, total_blocks)
            for t in range(QT + 1):
                rows, cols = (P, slice(t * P, (t + 1) * P)) if t < QT else (DEC_SEQ, slice(SEQ, TOK))
                if t >= 2:
                    pe.wait_ge(s_ye0, t - 1)
                    pe.wait_ge(s_ye1, t - 1)
                for half in range(2):
                    for c in range(4):
                        ins = turn(END_BANKS[t % 2][half][0:rows, c * P:(c + 1) * P], EN["y"][:, 4 * half + c, cols])
                    ins.then_inc(s_ym, 1)

        @block.gpsimd
        def _(pool):
            pool.memset(ident[:, :], 0.0).then_inc(s_p0, 1)
            pool.memset(flip[:, :], 0.0).then_inc(s_p0, 1)
            pool.memset(ST["tri_f"][:, :], 1.0).then_inc(s_p0, 1)
            pool.memset(ST["bias_rows"][:, :], 1.0).then_inc(s_p0, 1)
            pool.wait_ge(s_p0, 4)
            pool.affine_select(ident[:, :], ident[:, :], pattern=[[-1, P]], compare_op=ALU.not_equal, fill=1.0, base=0,
                               channel_multiplier=1).then_inc(s_cp, 1)
            pool.affine_select(flip[:, :], flip[:, :], pattern=[[1, P]], compare_op=ALU.not_equal, fill=1.0, base=-(P - 1),
                               channel_multiplier=1).then_inc(s_cp, 1)
            pool.affine_select(ST["tri_f"][:, :], ST["tri_f"][:, :], pattern=[[1, P]], compare_op=ALU.is_ge, fill=0.0, base=0,
                               channel_multiplier=-1).then_inc(s_p0, 1)
            pool.wait_ge(s_p0, 5)
            pool.memset(ST["tri_f"][0:CHUNK, CHUNK:P], 0.0).then_inc(s_p0, 1)
            pool.wait_ge(s_p0, 6)
            pool.tensor_copy(tri[:, :], ST["tri_f"][:, :]).then_inc(s_tri, 1)
            flat = SEQ - 1 - MAX_REL
            pool.dma_start(ST["rel_rev"][:, :], d["rel_rev"][:, 0:REL - 1]).then_inc(s_rel, 16)
            pool.wait_ge(s_rel, 16)
            pool.tensor_scalar(ST["bias_rows"][:, 0:flat], ST["bias_rows"][:, 0:flat], ST["rel_rev"][:, 0:1], None, ALU.mult)
            pool.tensor_copy(ST["bias_rows"][:, flat:flat + REL - 1], ST["rel_rev"][:, :]).then_inc(s_row, 1)
            pool.wait_ge(s_row, 1)
            pool.dma_start(bias_dram, ST["bias_rows"][:, :]).then_inc(s_bs, 16)
            pool.wait_ge(s_bs, 16)

            def x_square(m, n1, n2, stat, first=False, final=False):
                if first:
                    if not (isinstance(stat, int) and stat == 0):
                        pool.wait_ge(s_st1, stat)
                    pool.tensor_tensor(sq_sum[:, :], one(x, m), one(x, m), ALU.mult).then_inc(s_p2, 1)
                    return
                pool.wait_ge(s_p2, n2)
                pool.tensor_tensor(sq_one[:, :], one(x, m), one(x, m), ALU.mult).then_inc(s_p1, 1)
                pool.wait_ge(s_p1, n1 + 1)
                pool.tensor_tensor(sq_sum[:, :], sq_sum[:, :], sq_one[:, :], ALU.add).then_inc(s_sq if final else s_p2, 1)

            def x_norm_sum(n, stat, ready, b):
                n1, n2 = n * (XT - 1), n * (XT - 1)
                pool.wait_ge(ready, b + 1)
                x_square(0, n1, n2, stat, first=True)
                with pool.Fori(1, XT - 1) as m:
                    pool.wait_ge(ready, m + (b + 1))
                    x_square(m, m + (n1 - 1), m + n2, stat)
                pool.wait_ge(ready, b + XT)
                x_square(XT - 1, n1 + XT - 2, n2 + XT - 1, stat, final=True)
            x_norm_sum(0, 0, s_x0, 0)

            def gla(i, b0):
                gl, k0 = gla_no[i], stat_of[i, "head"]
                pool.wait_ge(s_mm, b0 + 1)
                pool.dma_start(GL["wb"][:, :], d[f"l{i}_gla_w_gate_b"]).then_inc(s_wb, 16)
                pool.wait_ge(s_wb, 16 * (gl + 1))

                def head(h):
                    b, q = b0 + 1 + h * 6, h + 4 * gl
                    pool.wait_ge(s_gm, q)
                    pool.tensor_copy(GL["wbh"][:, :], GL["wb"][:, ds(h * P, P)]).then_inc(s_wbh, 1)
                    pool.wait_ge(s_free, b + 2)
                    pool.wait_ge(s_e, q + 1)
                    pool.wait_ge(s_atm, q)
                    pool.tensor_tensor(GL["ke"][:, :], GL["k"][:, :], GL["enb"][:, :], ALU.mult).then_inc(s_ke, 1)
                    pool.wait_ge(s_ekd, q + 1)
                    pool.wait_ge(s_kdm, q)
                    pool.tensor_tensor(GL["kd"][:, :], GL["k"][:, :], GL["ekd"][:, :], ALU.mult).then_inc(s_kd, 1)
                    pool.wait_ge(s_oe, q + 1)
                    pool.wait_ge(s_st1, h + k0)
                    pool.tensor_tensor(sq_sum[:, :], GL["o"][:, 0, :], GL["o"][:, 0, :], ALU.mult)
                    pool.tensor_tensor(sq_one[:, :], GL["o"][:, 1, :], GL["o"][:, 1, :], ALU.mult).then_inc(s_hp, 1)
                    pool.wait_ge(s_hp, q + 1)
                    pool.tensor_tensor(sq_sum[:, :], sq_sum[:, :], sq_one[:, :], ALU.add).then_inc(s_sq, 1)
                head(0)
                with pool.Fori(1, GLA_HEADS) as h:
                    head(h)
                pool.wait_ge(s_sout, 32 * GLA_HEADS * (gl + 1))

            def attention(i, b0):
                pool.wait_ge(s_sq, stat_of[i, "mix"] + 1)
                for n, heads in enumerate((slice(0, 2), slice(2, ATT_HEADS))):
                    pool.wait_ge(s_bt[n], 16)
                    pool.memset(AT["bias"][CHUNK:P, heads, SEQ - CHUNK:SEQ], NEG_INF).then_inc(s_btm, 1)
                    pool.wait_ge(s_btm, n + 1)
                pool.wait_ge(s_kvo, 64 * PAIRS)

            def lru(i, b0):
                pool.wait_ge(s_mm, b0 + 1)
                pool.memset(LR["gate_w"][:, :, :, :], 0.0).then_inc(s_gw0, 1)
                pool.wait_ge(s_tlo, 64)

            n_sum = 1
            for i in range(layers):
                {"gla": gla, "att": attention, "lru": lru}[MIXERS[i]](i, base[i, "mix_in"])
                x_norm_sum(n_sum, stat_of[i, "ffn"], s_free, base[i, "mix_out"])
                x_norm_sum(n_sum + 1, stat_of[i + 1, "mix"] if i < last else stat_of["final"], s_free, base[i, "down1"])
                n_sum += 2


_OUTS = [(1, SEQ, D_MODEL), (1, DEC_SEQ, D_MODEL), (1, 4, 128, 256), (1, 4, 128, 256),
         (1, SEQ, ATT_HEADS, ATT_DH), (1, SEQ, ATT_HEADS, ATT_DH), (1, DEC_SEQ, ATT_HEADS, ATT_DH), (1, DEC_SEQ, ATT_HEADS, ATT_DH),
         (1, LRU_W), (1, CPAD, LRU_W), (1, LRU_W), (1, CPAD, LRU_W), (1, 4, 128, 256), (1, 4, 128, 256)]


def kernel(**inputs):
    import numpy as _np
    import concourse.bacc as _bacc
    from concourse import mybir as _mybir
    from concourse.bass_utils import run_bass_kernel_spmd as _run

    nc = _bacc.Bacc("TRN2", target_bir_lowering=False, num_devices=1)
    arrays, d = {}, {}
    for name, value in inputs.items():
        a = _np.ascontiguousarray(value)
        if name == "l1_att_rel_bias":
            name, a = "rel_rev", _np.ascontiguousarray(a[:, ::-1])
        arrays[f"in_{name}_dram"] = a
        d[name] = nc.dram_tensor(f"in_{name}_dram", a.shape, _mybir.dt.from_np(a.dtype), kind="ExternalInput").ap()
    o = [nc.dram_tensor(f"out_{i}_dram", shape, _mybir.dt.float32, kind="ExternalOutput").ap()
         for i, shape in enumerate(_OUTS)]
    encoder_step(nc, d, o)
    r = _run(nc, [arrays], core_ids=[0])
    return tuple(r.results[0][f"out_{i}_dram"] for i in range(len(_OUTS)))
```
